# Optimizing a Trainium2 kernel written in Bass

```python
import jax, jax.numpy as jnp
from jax import lax
import numpy as np

D_MODEL = 1024
BATCH = 1
SEQ = 512
DEPTH = 2
DEC_BATCH = 1
DEC_SEQ = 512
PAST_LEN = 128

N_MIXERS = 2
RMS_EPS = 1e-6
NEG_BIG = -1e30

A_GROUPS = ((128, 1), (512, 4), (2048, 16))
A_HEADS = 8
A_HEAD_DIM = 128
A_GROUP_WIDTH = A_HEADS * A_HEAD_DIM
A_BRANCH = A_GROUP_WIDTH
A_IN = len(A_GROUPS) * 3 * A_GROUP_WIDTH + A_BRANCH
ALIBI_MAX_EXP = 8.0

B_HEADS = 16
B_NOPE = 64
B_ROPE = 32
B_V = 64
B_Q_LORA = 384
B_KV_LORA = 256
B_BRANCH = B_HEADS * B_V
B_IN = B_Q_LORA + B_KV_LORA + B_ROPE + B_BRANCH
ROPE_THETA = 10000.0
Q_BLOCK = 128

kernel_name = "hybrid_dilated_mla_encoder"

def rms_norm(x, g):
    xf = x.astype(jnp.float32)
    y = xf * lax.rsqrt(jnp.mean(xf * xf, axis=-1, keepdims=True) + RMS_EPS)
    return (y * g.astype(jnp.float32)).astype(x.dtype)

def alibi_slopes(n):
    return (2.0 ** (-ALIBI_MAX_EXP * np.arange(1, n + 1) / n)).astype(np.float32)

def dilated_window_attention(q, k, v, slopes, window, dilation):
    B, S, H, dh = q.shape
    radius = (window // 2) // dilation
    blk = radius
    L = S // dilation
    nb = -(-L // blk)
    Lp = nb * blk

    def to_sub(t, pad_lo, pad_hi):
        t = t.reshape(B, L, dilation, H, dh).transpose(0, 2, 3, 1, 4)
        t = jnp.pad(t, ((0, 0), (0, 0), (0, 0), (pad_lo, pad_hi), (0, 0)))
        return t.reshape(B, dilation, H, -1, blk, dh)

    qb = to_sub(q, 0, Lp - L)
    kb = to_sub(k, blk, Lp - L + blk)
    vb = to_sub(v, blk, Lp - L + blk)
    scale = dh ** -0.5
    s = jnp.concatenate(
        [jnp.einsum('brhnqd,brhnkd->brhnqk', qb, kb[:, :, :, c:c + nb]) for c in range(3)],
        axis=-1).astype(jnp.float32) * scale

    i = np.arange(blk)[:, None]
    j = np.arange(3 * blk)[None, :]
    delta = j - blk - i
    u_q = np.arange(nb)[:, None, None] * blk + i[None]
    u_k = u_q + delta[None]
    valid = (np.abs(delta) <= radius)[None] & (u_k >= 0) & (u_k < L)
    bias = (-slopes[:, None, None] * (np.abs(delta) * dilation)[None]).astype(np.float32)
    s = s + jnp.asarray(bias)[:, None]
    s = jnp.where(jnp.asarray(valid), s, NEG_BIG)
    lse = jax.nn.logsumexp(s, axis=-1)
    p = jnp.exp(s - lse[..., None]).astype(v.dtype)
    o = sum(jnp.einsum('brhnqk,brhnkd->brhnqd', p[..., c * blk:(c + 1) * blk],
                       vb[:, :, :, c:c + nb]) for c in range(3))

    def from_sub(t):
        t = t.reshape(B, dilation, H, Lp, -1)[:, :, :, :L]
        return t.transpose(0, 3, 1, 2, 4).reshape(B, S, H, -1)

    return from_sub(o), from_sub(lse[..., None])[..., 0]

def dilated_mixer(h, w_in, w_out):
    B, S, _ = h.shape
    proj = h @ w_in
    gw = A_GROUP_WIDTH
    slopes = alibi_slopes(len(A_GROUPS) * A_HEADS).reshape(len(A_GROUPS), A_HEADS)
    outs, lses = [], []
    for g, (window, dil) in enumerate(A_GROUPS):
        base = 3 * gw * g
        q, k, v = (proj[..., base + n * gw: base + (n + 1) * gw].reshape(B, S, A_HEADS, A_HEAD_DIM)
                   for n in range(3))
        o, lse = dilated_window_attention(q, k, v, slopes[g], window, dil)
        outs.append(o)
        lses.append(lse)
    wts = jax.nn.softmax(jnp.stack(lses), axis=0)
    o = jnp.sum(wts[..., None] * jnp.stack(outs).astype(jnp.float32), axis=0)
    gate = proj[..., -A_BRANCH:]
    y = o.reshape(B, S, A_BRANCH).astype(h.dtype) * jax.nn.silu(gate)
    return y @ w_out

def rope_tables(S):
    inv_freq = (ROPE_THETA ** (-np.arange(0, B_ROPE, 2) / B_ROPE)).astype(np.float32)
    ang = jnp.arange(S, dtype=jnp.float32)[:, None] * jnp.asarray(inv_freq)[None, :]
    return jnp.cos(ang), jnp.sin(ang)

def apply_rope(x, cos, sin):
    xf = x.astype(jnp.float32)
    half = xf.shape[-1] // 2
    x1, x2 = xf[..., :half], xf[..., half:]
    c, s = cos[None, :, None, :], sin[None, :, None, :]
    return jnp.concatenate([x1 * c - x2 * s, x1 * s + x2 * c], axis=-1).astype(x.dtype)

def blockwise_attention(q, k, v):
    B, S, H, dq = q.shape
    scale = dq ** -0.5
    qb = q.reshape(B, S // Q_BLOCK, Q_BLOCK, H, dq).transpose(1, 0, 2, 3, 4)

    def one_block(qblk):
        s = jnp.einsum('bqhd,bkhd->bhqk', qblk, k).astype(jnp.float32) * scale
        p = jax.nn.softmax(s, axis=-1).astype(v.dtype)
        return jnp.einsum('bhqk,bkhd->bqhd', p, v)

    o = lax.map(one_block, qb)
    return o.transpose(1, 0, 2, 3, 4).reshape(B, S, H, -1)

def mla_mixer(h, w_in, q_norm_g, w_q_up, kv_norm_g, w_kv_up, w_out):
    B, S, _ = h.shape
    proj = h @ w_in
    c_q, c_kv, k_rope, gate = jnp.split(
        proj, [B_Q_LORA, B_Q_LORA + B_KV_LORA, B_Q_LORA + B_KV_LORA + B_ROPE], axis=-1)
    q = (rms_norm(c_q, q_norm_g) @ w_q_up).reshape(B, S, B_HEADS, B_NOPE + B_ROPE)
    kv = (rms_norm(c_kv, kv_norm_g) @ w_kv_up).reshape(B, S, B_HEADS, B_NOPE + B_V)
    cos, sin = rope_tables(S)
    q_rope = apply_rope(q[..., B_NOPE:], cos, sin)
    k_rope = apply_rope(k_rope[:, :, None, :], cos, sin)
    qf = jnp.concatenate([q[..., :B_NOPE], q_rope], axis=-1)
    kf = jnp.concatenate([kv[..., :B_NOPE], jnp.broadcast_to(k_rope, (B, S, B_HEADS, B_ROPE))], axis=-1)
    o = blockwise_attention(qf, kf, kv[..., B_NOPE:])
    y = o.reshape(B, S, B_BRANCH) * jax.nn.silu(gate)
    return y @ w_out

def encoder_trunk(x, norm_g, a_w_in, a_w_out, b_w_in, b_q_norm_g, b_w_q_up,
                  b_kv_norm_g, b_w_kv_up, b_w_out, final_norm_g):
    for i in range(DEPTH):
        h = rms_norm(x, norm_g[i])
        j = i // N_MIXERS
        if i % N_MIXERS == 0:
            y = dilated_mixer(h, a_w_in[j], a_w_out[j])
        else:
            y = mla_mixer(h, b_w_in[j], b_q_norm_g[j], b_w_q_up[j],
                          b_kv_norm_g[j], b_w_kv_up[j], b_w_out[j])
        x = x + y
    return rms_norm(x, final_norm_g)

def setup_inputs(seed: int = 0) -> dict:
    key = jax.random.key(seed)
    ks = jax.random.split(key, 13)
    n_a = (DEPTH + 1) // 2
    n_b = DEPTH // 2
    f32 = jnp.float32

    def nrm(k, shape, scale):
        return jax.random.normal(k, shape, f32) * scale

    return {
        "x_prompt": nrm(ks[0], (BATCH, SEQ, D_MODEL), 1.0),
        "x_sample": nrm(ks[1], (DEC_BATCH, DEC_SEQ, D_MODEL), 1.0),
        "norm_g": 1.0 + nrm(ks[2], (DEPTH, D_MODEL), 0.01),
        "a_w_in": nrm(ks[3], (n_a, D_MODEL, A_IN), D_MODEL ** -0.5),
        "a_w_out": nrm(ks[4], (n_a, A_BRANCH, D_MODEL), A_BRANCH ** -0.5),
        "b_w_in": nrm(ks[5], (n_b, D_MODEL, B_IN), D_MODEL ** -0.5),
        "b_q_norm_g": 1.0 + nrm(ks[6], (n_b, B_Q_LORA), 0.01),
        "b_w_q_up": nrm(ks[7], (n_b, B_Q_LORA, B_HEADS * (B_NOPE + B_ROPE)), B_Q_LORA ** -0.5),
        "b_kv_norm_g": 1.0 + nrm(ks[8], (n_b, B_KV_LORA), 0.01),
        "b_w_kv_up": nrm(ks[9], (n_b, B_KV_LORA, B_HEADS * (B_NOPE + B_V)), B_KV_LORA ** -0.5),
        "b_w_out": nrm(ks[10], (n_b, B_BRANCH, D_MODEL), B_BRANCH ** -0.5),
        "final_norm_g": 1.0 + nrm(ks[11], (D_MODEL,), 0.01),
    }

def reference(x_prompt, x_sample, norm_g, a_w_in, a_w_out, b_w_in, b_q_norm_g,
              b_w_q_up, b_kv_norm_g, b_w_kv_up, b_w_out, final_norm_g):
    y_prompt = encoder_trunk(x_prompt, norm_g, a_w_in, a_w_out, b_w_in, b_q_norm_g,
                             b_w_q_up, b_kv_norm_g, b_w_kv_up, b_w_out, final_norm_g)
    y_sample = encoder_trunk(x_sample, norm_g, a_w_in, a_w_out, b_w_in, b_q_norm_g,
                             b_w_q_up, b_kv_norm_g, b_w_kv_up, b_w_out, final_norm_g)
    return (y_prompt, y_sample)


_drawn_inputs = setup_inputs


def setup_inputs(seed=0):
    import zlib

    import numpy as np

    out = dict(_drawn_inputs(seed))
    spreads = {}
    factors = {'norm_g': 8.0, 'b_q_norm_g': 8.0, 'b_kv_norm_g': 8.0, 'final_norm_g': 5.65}
    for name, (base, spread) in spreads.items():
        noise = np.random.default_rng([zlib.crc32(name.encode()), seed]).standard_normal(out[name].shape)
        drawn = base * np.exp(spread * noise) if base else spread * noise
        out[name] = __import__('jax').numpy.asarray(drawn.astype(out[name].dtype))
    for name, factor in factors.items():
        out[name] = (out[name] * factor).astype(out[name].dtype)
    return out
```

```python
from contextlib import ExitStack

import concourse.bass as bass
from concourse import mybir

F32 = mybir.dt.float32
F32R = mybir.dt.float32r
ALU = mybir.AluOpType
ACT = mybir.ActivationFunctionType
AX = mybir.AxisListType

P = 128
D = 1024
KT = D // P
S = 512
NB = 2
QT = S // P
NT = NB * QT
HALF = D // 2
RMS_EPS = 1e-6

A_HEADS = 8
A_DIM = 128
A_SCALE = float(A_DIM) ** -0.5

HI, LO = 0, 1
SPLIT_PRODUCT = ((HI, HI), (HI, LO), (LO, HI))

PROJ = ["q0", "k0", "v0", "q1", "k1", "v1", "gate", "q2", "k2", "v2"]
BLOCKS = ["q0", "k0", "v0", "q1", "k1", "out0", "out1", "v1", "gate", "q2", "k2", "v2"]


OUTPUTS = ["out0", "out1"]


def is_first(h):
    return isinstance(h, int) and h == 0


def is_past(h):
    return isinstance(h, int) and h == A_HEADS


def names(h):
    return PROJ if is_first(h) else OUTPUTS if is_past(h) else BLOCKS


def block_no(h, name):
    return names(h).index(name) + (0 if is_first(h) else h * len(BLOCKS) - 2)


def block_slot(h, name):
    return names(h).index(name) % 2


def proj_no(h, name):
    return h * len(PROJ) + PROJ.index(name)


NORM_TURNS = NB * KT
TURNS = {"v2": 0, "p": 2, "v0": 10, "v1": 12}
TURNS_FIRST = {"v0": 0, "v1": 2}


def turn_no(h, kind, n):
    if is_first(h):
        return NORM_TURNS + TURNS_FIRST[kind] + n
    return h * 14 + NORM_TURNS - 10 + TURNS[kind] + n


SUMS = {"s0": 0, "out": 4, "s1": 20, "s2": 22}
SUMS_FIRST = {"s0": 0, "s1": 4, "s2": 6}
SUMS_PAST = {"out": 0}


def sum_table(h):
    return SUMS_FIRST if is_first(h) else SUMS_PAST if is_past(h) else SUMS


def sum_no(h, kind, n):
    return sum_table(h)[kind] + n + (0 if is_first(h) else h * 24 - 16)


def sum_slot(h, kind, n):
    return (sum_table(h)[kind] + n) % 2


def turn_slot(h, kind, n):
    return ((TURNS_FIRST if is_first(h) else TURNS)[kind] + n) % 2


def key_chunk(v, c):
    if c in (0, QT):
        return v.rearrange("p (j s w) -> p s j w", j=QT, w=16)[:, 0:8:7]
    return v.rearrange("p (j u) -> p j u", j=QT)[:, :, 32 * c - 16:32 * c + 16]


def block_major(v, ps):
    return v.rearrange("p (t j w) -> p j t w", t=QT, j=QT), ps.rearrange("p (j t w) -> p j t w", t=QT, j=QT)


def chunk_major(v, ps):
    inner = (v[:, P:].rearrange("p (c j w) -> p j c w", c=QT - 1, j=QT),
             ps.rearrange("p (j u) -> p j u", j=QT)[:, :, 16:P - 16].rearrange("p j (c w) -> p j c w", w=32))
    ends = (v[:, 0:P].rearrange("p (s j w) -> p s j w", s=2, j=QT), key_chunk(ps, 0))
    return inner, ends


BETWEEN = {
    ("q0", 0): (("v2", 0), ("v2", 1)),
    ("q0", 1): (("turn", 0, 0), ("turn", 0, 1)),
    ("k0", 0): (("weigh", 0, 0), ("turn", 0, 2), ("weigh", 0, 1), ("turn", 0, 3)),
    ("k0", 1): (("weigh", 0, 2), ("weigh", 0, 3), ("turn", 1, 0), ("turn", 1, 1)),
    ("v0", 0): (("weigh", 1, 0), ("turn", 1, 2), ("weigh", 1, 1), ("turn", 1, 3)),
    ("v0", 1): (("weigh", 1, 2), ("weigh", 1, 3)),
}
GATED = {("k0", 1): 0, ("v0", 1): 1}
DVE_STEPS = 14

CHUNK_QUERIES = {1: ((0, 1), (1, 0)), 2: ((1, 1), (2, 0)), 3: ((2, 1), (3, 0)), 0: ((0, 0), (3, 1))}


def stage_a(nc, io, X, ident, eps_pow):
    with ExitStack() as ctx:
        def sb(name, shape, dt=F32):
            return ctx.enter_context(nc.sbuf_tensor(name, shape, dt))

        def sem(name):
            return ctx.enter_context(nc.semaphore(name))

        hT = [sb(f"hT{s}", [P, KT, NB * S], F32R) for s in "hl"]
        qk = [sb(f"qk{s}", [P, 2, NB, S], F32R) for s in "hl"]
        val = [sb(f"val{s}", [P, 3, NB, QT, A_DIM], F32R) for s in "hl"]
        vT = sb("vT", [P, NB, S])
        prob = sb("prob", [P, 2, NB, QT, 2 * P])
        pT = [sb(f"pT{s}", [P, 2, S], F32R) for s in "hl"]
        gate = sb("gate", [P, NB, S])
        y = sb("y", [P, S])
        yT = [sb(f"yT{s}", [P, NB, S], F32R) for s in "hl"]
        raw = sb("raw", [P, 2, KT * P])
        w = [sb(f"w{s}", [P, 2, KT * P], F32R) for s in "hl"]
        bias = sb("bias", [P, 8 * P])
        g_col = sb("g_col", [P, KT])
        ss = sb("ss", [P, NT])
        ms = sb("ms", [P, NT])
        rstd = sb("rstd", [P, NT])
        st_blk = sb("st_blk", [P, NB, QT, 2])
        st_tile = sb("st_tile", [P, NB, QT, 2])
        st_dil = sb("st_dil", [P, NB, QT, 2])
        negmax = sb("negmax", [P, 2, NB, QT])
        joint = sb("joint", [P, NB, QT])
        fac = sb("fac", [P, 2, NB, QT])
        den = sb("den", [P, 2, NB, QT])
        wt = sb("wt", [P, 2, NB, QT])
        wt_blk = sb("wt_blk", [P, NB, QT])

        bank = [ctx.enter_context(nc.psum_tensor(f"bankA{i}", [P, S], F32)) for i in range(8)]
        proj_ps, sum_ps, turn_ps, out_ps = bank[0:2], bank[2:4], bank[4:6], bank[6:8]

        x_loaded = [sem(f"x_loaded{b}") for b in range(NB)]
        g_loaded = sem("g_loaded")
        squared = sem("squared")
        mean_ready = sem("mean_ready")
        rstd_ready = sem("rstd_ready")
        x_scaled = sem("x_scaled")
        raw_loaded = [sem(f"raw_loaded{i}") for i in range(2)]
        bias_loaded = sem("bias_loaded")
        w_hi = sem("w_hi")
        w_split = sem("w_split")
        proj_done = [sem(f"proj_done{b}") for b in range(NB)]
        proj_hi = sem("proj_hi")
        proj_taken = [sem(f"proj_taken{b}") for b in range(NB)]
        gate_exp = sem("gate_exp")
        turned = sem("turned")
        turn_hi = sem("turn_hi")
        turn_taken = sem("turn_taken")
        sum_done = sem("sum_done")
        sum_taken = sem("sum_taken")
        negmax_ready = sem("negmax_ready")
        exp_done = sem("exp_done")
        fac_in = sem("fac_in")
        fac_ready = sem("fac_ready")
        prob_ready = sem("prob_ready")
        o_done = sem("o_done")
        y_ready = sem("y_ready")
        y_hi = sem("y_hi")
        y_split = sem("y_split")
        dve_step = sem("dve_step")

        block = ctx.enter_context(nc.Block())
        scaled_x = prob[:].rearrange("p g b t k -> p (g b) (t k)")

        @block.sync
        def _(sp):
            for b, name in enumerate(("x_prompt", "x_sample")):
                src = io[name][0].rearrange("(u j) d -> u j d", j=QT)
                sp.dma_start(X[:, b * QT:(b + 1) * QT, :], src).then_inc(x_loaded[b], 16)
                if b == 0:
                    sp.dma_start(g_col[:, :], io["norm_g"][0]).then_inc(g_loaded, 16)

            def load_block(h, name):
                n = block_no(h, name)
                slot = block_slot(h, name)
                if not (is_first(h) and PROJ.index(name) < 2):
                    sp.wait_ge(w_split, n - 1)
                if name.startswith("out"):
                    half = int(name[3]) * HALF
                    src = io["a_w_out"][bass.ds(h - 1, 1), :, half:half + HALF].rearrange("o p c -> (o p) c")
                    dst = raw[:, slot, 0:HALF]
                else:
                    at = ["q0", "k0", "v0", "q1", "k1", "v1", "q2", "k2", "v2", "gate"].index(name)
                    src = io["a_w_in"][bass.ds(h, 1), at].rearrange("o p c -> (o p) c")
                    dst = raw[:, slot, :]
                sp.dma_start(dst, src).then_inc(raw_loaded[slot], 16)

            def load_bias(h):
                if not is_first(h):
                    sp.wait_ge(sum_taken, sum_no(h, "s0", 0))
                sp.dma_start(bias[:, :], io["alibi"][bass.ds(h, 1)].rearrange("o p c -> (o p) c")
                             ).then_inc(bias_loaded, 16)

            for name in PROJ:
                load_block(0, name)
                if name == "q0":
                    load_bias(0)
            with sp.Fori(1, A_HEADS) as h:
                for n, name in enumerate(BLOCKS):
                    load_block(h, name)
                    if n == 1:
                        load_bias(h)
            load_block(A_HEADS, "out0")
            load_block(A_HEADS, "out1")

        @block.gpsimd
        def _(pool):
            pool.wait_ge(mean_ready, 1)
            pool.tensor_tensor(rstd[:, :], ms[:, :], eps_pow[:, :], ALU.pow).then_inc(rstd_ready, 1)

        @block.scalar
        def _(act):
            for b in range(NB):
                act.wait_ge(x_loaded[b], 16)
                for j in range(QT):
                    i = b * QT + j
                    act.activation(hT[LO][:, j, :] if b else scaled_x[:, j, :], X[:, i, :], ACT.Square,
                                   accum_out=ss[:, i:i + 1]).then_inc(squared, 1)

            def split_weights(h, name):
                k, slot = names(h).index(name), block_slot(h, name)
                act.wait_ge(raw_loaded[slot], 16 * (k // 2 + 1) if is_first(h) else h * 96 + 16 * (k // 2))
                if k >= 2 and names(h)[k - 2].startswith("out"):
                    half = int(names(h)[k - 2][3])
                    act.wait_ge(sum_done, sum_no(h, "out", (half + 1) * NT - 1) + 1)
                elif k >= 2:
                    act.wait_ge(proj_done[1], proj_no(h, names(h)[k - 2]) + 1)
                elif not is_first(h):
                    act.wait_ge(proj_done[1], h * len(PROJ) - 1 + k)
                act.activation(w[HI][:, slot, :], raw[:, slot, :], ACT.Copy).then_inc(w_hi, 1)

            def turn(h, kind, n, dst):
                at = turn_no(h, kind, n)
                slot = turn_slot(h, kind, n)
                act.wait_ge(turned, at + 1)
                act.activation(dst(slot, HI), turn_ps[slot][:, :], ACT.Copy).then_inc(turn_hi, 1)

            def take(h, name, b):
                n = proj_no(h, name)
                act.wait_ge(proj_done[b], n + 1)
                ps = proj_ps[b][:, :]
                if name[0] in "qk":
                    g = int(name[1])
                    if g:
                        act.wait_ge(sum_done, sum_no(h, f"s{g - 1}", 3 if g == 1 else 1) + 1)
                    elif not is_first(h):
                        act.wait_ge(sum_done, h * 24 - 16)
                    dst = qk[HI][:, "qk".index(name[0]), b, :]
                    if name == "q0":
                        dst, ps = block_major(dst, ps)
                    act.activation(dst, ps, ACT.Copy).then_inc(proj_hi, 1)
                elif name[0] == "v":
                    if name == "v0":
                        (d0, s0), (d1, s1) = chunk_major(vT[:, b, :], ps)
                        act.activation(d0, s0, ACT.Copy)
                        act.activation(d1, s1, ACT.Copy).then_inc(proj_taken[b], 1)
                    else:
                        act.activation(vT[:, b, :], ps, ACT.Copy).then_inc(proj_taken[b], 1)
                else:
                    if not is_first(h):
                        act.wait_ge(y_ready, h * 2)
                    act.activation(gate[:, b, :], ps, ACT.Exp, scale=-1.0).then_inc(gate_exp, 1)

            def exps(h, g, bs):
                for b in bs:
                    act.wait_ge(negmax_ready, h * 3 + 1 + (0 if g == 0 else 1 + b))
                    st = st_blk if g == 0 else st_dil
                    for t in range(QT):
                        ins = act.activation(prob[:, g, b, t, :], prob[:, g, b, t, :], ACT.Exp,
                                             bias=negmax[:, g, b, t:t + 1], scale=A_SCALE,
                                             accum_out=st[:, b, t, 1:2])
                    if not (g == 0 and b == 0):
                        ins.then_inc(exp_done, 1)

            def factors(h):
                act.wait_ge(fac_in, h + 1)
                act.activation(fac[:, :, :, :], fac[:, :, :, :], ACT.Exp, scale=A_SCALE).then_inc(fac_ready, 1)

            for n, name in enumerate(PROJ[:2]):
                split_weights(0, name)
            act.wait_ge(g_loaded, 16)
            for b in range(NB):
                for k in range(KT):
                    n = b * KT + k
                    act.wait_ge(turned, n + 1)
                    act.activation(hT[HI][:, k, b * S:(b + 1) * S], turn_ps[n % 2][:, :], ACT.Copy,
                                   scale=g_col[:, k:k + 1]).then_inc(turn_hi, 1)

            def next_split(h, name):
                k = names(h).index(name) + 2
                if k < len(names(h)):
                    split_weights(h, names(h)[k])
                else:
                    split_weights(h + 1, BLOCKS[k - len(names(h))])

            def head(h):
                for name in names(h):
                    for b in range(NB):
                        if name in PROJ:
                            take(h, name, b)
                        if not is_first(h):
                            between(h, name, b)
                        if name == "v2" and b == 0:
                            exps(h, 1, [1])
                    if name in ("v0", "v1"):
                        for b in range(NB):
                            turn(h, name, b, lambda slot, part, b=b, g=int(name[1]): val[part][:, g, b])
                    next_split(h, name)
                    if name == "v0":
                        exps(h, 0, [0, 1])
                    if name == "k2":
                        exps(h, 1, [0])
                factors(h)

            def between(h, name, b):
                for step in BETWEEN.get((name, b), ()):
                    if step[0] == "v2":
                        turn(h, "v2", step[1], lambda slot, part, g=step[1]: val[part][:, 2, g])
                    elif step[0] == "turn":
                        turn(h, "p", 4 * step[1] + step[2], lambda slot, part: pT[part][:, slot, :])
                if (name, b) in GATED:
                    yb = GATED[name, b]
                    act.wait_ge(y_ready, h * 2 - 1 + yb)
                    act.activation(yT[HI][:, yb, :], y[:, :], ACT.Copy).then_inc(y_hi, 1)

            head(0)
            with act.Fori(1, A_HEADS) as h:
                head(h)
            for name in ("q0", "k0", "v0"):
                for b in range(NB):
                    between(A_HEADS, name, b)

        @block.vector
        def _(dve):
            for b in range(NB):
                dve.wait_ge(squared, (b + 1) * QT)
            dve.tensor_scalar(ms[:, :], ss[:, :], 1.0 / D, RMS_EPS, ALU.mult, ALU.add).then_inc(mean_ready, 1)
            dve.wait_ge(rstd_ready, 1)
            for b in range(NB):
                if b:
                    dve.wait_ge(turned, KT * b)
                for j in range(QT):
                    i = b * QT + j
                    ins = dve.tensor_scalar(scaled_x[:, j, :], X[:, i, :], rstd[:, i:i + 1], None, ALU.mult)
                ins.then_inc(x_scaled, 1)
                if b == 0:
                    dve.wait_ge(g_loaded, 16)
                    for n in range(2):
                        dve.wait_ge(w_hi, n + 1)
                        dve.tensor_tensor(w[LO][:, n, :], raw[:, n, :], w[HI][:, n, :],
                                          ALU.subtract).then_inc(w_split, 1)
                for k in range(KT):
                    n = b * KT + k
                    cols = slice(b * S, (b + 1) * S)
                    dve.wait_ge(turn_hi, n + 1)
                    dve.scalar_tensor_tensor(hT[LO][:, k, cols], turn_ps[n % 2][:, :], g_col[:, k:k + 1],
                                             hT[HI][:, k, cols], ALU.mult, ALU.subtract).then_inc(turn_taken, 1)

            def split_weights(h, name):
                slot = block_slot(h, name)
                dve.wait_ge(w_hi, block_no(h, name) + 1)
                dve.tensor_tensor(w[LO][:, slot, :], raw[:, slot, :], w[HI][:, slot, :],
                                  ALU.subtract).then_inc(w_split, 1)

            def turn(h, kind, n, dst):
                at = turn_no(h, kind, n)
                slot = turn_slot(h, kind, n)
                dve.wait_ge(turn_hi, at + 1)
                dve.tensor_tensor(dst(slot, LO), turn_ps[slot][:, :], dst(slot, HI),
                                  ALU.subtract).then_inc(turn_taken, 1)

            def chain(ins, h, n):
                ins.then_inc(dve_step, 1)
                dve.wait_ge(dve_step, h * DVE_STEPS + n + 1)

            def take(h, name, b):
                ps = proj_ps[b][:, :]
                if name[0] in "qk":
                    g, which = int(name[1]), "qk".index(name[0])
                    dve.wait_ge(proj_hi, h * 12 + 4 * g + 2 * which + b + 1)
                    hi, lo = qk[HI][:, which, b, :], qk[LO][:, which, b, :]
                    if name == "q0":
                        hi, _ = block_major(hi, ps)
                        lo, ps = block_major(lo, ps)
                    dve.tensor_tensor(lo, ps, hi, ALU.subtract).then_inc(proj_taken[b], 1)
                elif name == "gate":
                    dve.wait_ge(gate_exp, h * 2 + b + 1)
                    gb = gate[:, b, :]
                    chain(dve.tensor_scalar(gb, gb, 1.0, None, ALU.add), h, 1 + 2 * b)
                    chain(dve.reciprocal(gb, gb), h, 2 + 2 * b)
                    dve.tensor_tensor(gb, ps, gb, ALU.mult).then_inc(proj_taken[b], 1)

            def take_scores(h, kind, n):
                at = sum_no(h, kind, n)
                slot = sum_slot(h, kind, n)
                dve.wait_ge(sum_done, at + 1)
                g = int(kind[1])
                if g == 0:
                    b, pair = n // 2, n % 2
                    dst = prob[:, 0, b, 2 * pair:2 * pair + 2, :].rearrange("p t k -> p (t k)")
                    src = bias[:, 2 * P * pair:2 * P * pair + 4 * P]
                    ps = sum_ps[slot][:, :]
                else:
                    dst = prob[:, 1, n, :, (g - 1) * P:g * P]
                    src = bias[:, (5 + g) * P:(6 + g) * P].unsqueeze(1).broadcast_to((P, QT, P))
                    ps = sum_ps[slot][:].rearrange("p (t k) -> p t k", t=QT)
                dve.tensor_tensor(dst, ps, src, ALU.add).then_inc(sum_taken, 1)
                return at

            def maxima(h, g, bs, at, n):
                dve.wait_ge(sum_taken, at + 1)
                st = (st_blk if g == 0 else st_dil)[:, bs, :, 0]
                chain(dve.tensor_reduce(st, prob[:, g, bs, :, :], AX.X, ALU.max), h, n)
                dve.tensor_scalar(negmax[:, g, bs, :], st, -A_SCALE, None, ALU.mult).then_inc(negmax_ready, 1)

            def joint_softmax(h):
                dve.wait_ge(exp_done, (h + 1) * 3)
                for s in range(4):
                    for d in range(4):
                        ins = dve.tensor_copy(st_tile[32 * d:32 * d + 32, :, s, :], st_blk[32 * s:32 * s + 32, :, d, :])
                chain(ins, h, 7)
                chain(dve.tensor_tensor(joint[:], st_tile[:, :, :, 0], st_dil[:, :, :, 0], ALU.max), h, 8)
                dve.tensor_tensor(fac[:, 0], st_tile[:, :, :, 0], joint[:], ALU.subtract)
                dve.tensor_tensor(fac[:, 1], st_dil[:, :, :, 0], joint[:], ALU.subtract).then_inc(fac_in, 1)
                dve.wait_ge(fac_ready, h + 1)
                dve.tensor_tensor(den[:, 0], fac[:, 0], st_tile[:, :, :, 1], ALU.mult)
                chain(dve.tensor_tensor(den[:, 1], fac[:, 1], st_dil[:, :, :, 1], ALU.mult), h, 9)
                chain(dve.tensor_tensor(den[:, 0], den[:, 0], den[:, 1], ALU.add), h, 10)
                chain(dve.reciprocal(den[:, 1], den[:, 0]), h, 11)
                dve.tensor_tensor(wt[:, 0], fac[:, 0], den[:, 1], ALU.mult)
                chain(dve.tensor_tensor(wt[:, 1], fac[:, 1], den[:, 1], ALU.mult), h, 12)
                for s in range(4):
                    for d in range(4):
                        ins = dve.tensor_copy(wt_blk[32 * s:32 * s + 32, :, d], wt[32 * d:32 * d + 32, 0, :, s])
                chain(ins, h, 13)
                for b in range(NB):
                    for g in range(2):
                        for t in range(QT):
                            scale = wt_blk[:, b, t:t + 1] if g == 0 else wt[:, 1, b, t:t + 1]
                            ins = dve.tensor_scalar(prob[:, g, b, t, :], prob[:, g, b, t, :], scale, None, ALU.mult)
                    ins.then_inc(prob_ready, 1)

            def add_output(h, name):
                for n in range(NT):
                    k = int(name[3]) * NT + n
                    at = sum_no(h, "out", k)
                    slot = sum_slot(h, "out", k)
                    cols = slice(int(name[3]) * HALF, (int(name[3]) + 1) * HALF)
                    dve.wait_ge(sum_done, at + 1)
                    dve.tensor_tensor(X[:, n, cols], sum_ps[slot][:, :], X[:, n, cols], ALU.add).then_inc(sum_taken, 1)

            def between(h, name, b):
                for step in BETWEEN.get((name, b), ()):
                    if step[0] == "v2":
                        turn(h, "v2", step[1], lambda slot, part, g=step[1]: val[part][:, 2, g])
                    elif step[0] == "turn":
                        turn(h, "p", 4 * step[1] + step[2], lambda slot, part: pT[part][:, slot, :])
                if (name, b) in GATED:
                    yb = GATED[name, b]
                    dve.wait_ge(o_done, h * 2 - 1 + yb)
                    dve.tensor_tensor(y[:, :], out_ps[yb][:, :], gate[:, yb, :], ALU.mult).then_inc(y_ready, 1)
                    dve.wait_ge(y_hi, h * 2 - 1 + yb)
                    dve.tensor_tensor(yT[LO][:, yb, :], y[:, :], yT[HI][:, yb, :], ALU.subtract).then_inc(y_split, 1)

            def next_split(h, name):
                k = names(h).index(name) + 2
                if k < len(names(h)):
                    split_weights(h, names(h)[k])
                else:
                    split_weights(h + 1, BLOCKS[k - len(names(h))])

            def head(h):
                for name in names(h):
                    if name in OUTPUTS:
                        add_output(h, name)
                    for b in range(NB):
                        if name in PROJ:
                            take(h, name, b)
                        if not is_first(h):
                            between(h, name, b)
                        if (name, b) in (("k2", 1), ("v2", 0)):
                            at = take_scores(h, "s2", 1 - b)
                            maxima(h, 1, slice(1 - b, 2 - b), at, 6 - b)
                    if name == "v0":
                        for n in range(4):
                            at = take_scores(h, "s0", n)
                    if name == "v1":
                        for b in range(NB):
                            take_scores(h, "s1", b)
                    if name in ("v0", "v1"):
                        for b in range(NB):
                            turn(h, name, b, lambda slot, part, b=b, g=int(name[1]): val[part][:, g, b])
                    next_split(h, name)
                    if name == "v0":
                        maxima(h, 0, slice(0, NB), at, 0)
                joint_softmax(h)

            head(0)
            with dve.Fori(1, A_HEADS) as h:
                head(h)
            for name in ("q0", "k0", "v0"):
                for b in range(NB):
                    between(A_HEADS, name, b)
            for name in ("out0", "out1"):
                add_output(A_HEADS, name)

        @block.tensor
        def _(pe):
            for b in range(NB):
                pe.wait_ge(x_scaled, b + 1)
                for k in range(KT):
                    n = b * KT + k
                    if n >= 2:
                        pe.wait_ge(turn_taken, n - 1)
                    for j in range(QT):
                        ins = pe.transpose(turn_ps[n % 2][:, j * P:(j + 1) * P],
                                           scaled_x[:, j, k * P:(k + 1) * P], ident[:, :])
                    ins.then_inc(turned, 1)

            def project(h, name, b):
                n, p = block_no(h, name), proj_no(h, name)
                slot = block_slot(h, name)
                pe.wait_ge(w_split, n + 1)
                if not (is_first(h) and name == "q0"):
                    pe.wait_ge(proj_taken[b], p)
                last = KT * len(SPLIT_PRODUCT) - 1
                i = 0
                for k in range(KT):
                    if is_first(h) and name == "q0":
                        pe.wait_ge(turn_taken, b * KT + k + 1)
                    for a, c in SPLIT_PRODUCT:
                        ins = pe.matmul(proj_ps[b][:, :], w[a][:, slot, k * P:(k + 1) * P],
                                        hT[c][:, k, b * S:(b + 1) * S], start=(i == 0), stop=(i == last))
                        i += 1
                ins.then_inc(proj_done[b], 1)

            def turn(h, kind, n, tiles):
                at = turn_no(h, kind, n)
                slot = turn_slot(h, kind, n)
                pe.wait_ge(turn_taken, at - 1)
                for i, tile in enumerate(tiles):
                    ins = pe.transpose(turn_ps[slot][:, i * P:(i + 1) * P], tile, ident[:, :])
                ins.then_inc(turned, 1)

            def turn_values(h, g, b, at_head):
                pe.wait_ge(proj_taken[b], proj_no(at_head, f"v{g}") + 1)
                turn(h, f"v{g}", b, [vT[:, b, j * P:(j + 1) * P] for j in range(QT)])

            def turn_probs(h, b, part):
                if part == 0:
                    pe.wait_ge(prob_ready, h * 2 - 1 + b)
                if part < 2:
                    tiles = [prob[:, 0, b, t, half * P:(half + 1) * P]
                             for c in ((1, 2), (3, 0))[part] for t, half in CHUNK_QUERIES[c]]
                else:
                    tiles = [prob[:, 1, b, t, (part - 2) * P:(part - 1) * P] for t in range(QT)]
                turn(h, "p", 4 * b + part, tiles)

            def weigh_values(h, b, part):
                at = turn_no(h, "p", 4 * b + part)
                slot = part % 2
                pe.wait_ge(turn_taken, at + 1)
                o = out_ps[b][:, :]
                if part < 2:
                    for i, c in enumerate(((1, 2), (3, 0))[part]):
                        t0, t1 = (t for t, _ in CHUNK_QUERIES[c])
                        dst = o.rearrange("p (j s w) -> p s j w", j=QT, w=32)[:, t0:t1 + 1:t1 - t0]
                        for m, (a, d) in enumerate(SPLIT_PRODUCT):
                            pe.matmul(dst, val[a][:, 0, b, c, :], pT[d][:, slot, i * 2 * P:(i + 1) * 2 * P],
                                      start=(part == 0 and i == 0 and m == 0), stop=False, skip_group_check=True)
                else:
                    for t in range(QT):
                        for m, (a, d) in enumerate(SPLIT_PRODUCT):
                            ins = pe.matmul(o[:, t * P:(t + 1) * P], val[a][:, part - 1, b, t, :],
                                            pT[d][:, slot, t * P:(t + 1) * P], start=False,
                                            stop=(part == 3 and m == 2), skip_group_check=True)
                    if part == 3:
                        ins.then_inc(o_done, 1)

            def score(h, kind, n):
                at = sum_no(h, kind, n)
                slot = sum_slot(h, kind, n)
                if not (is_first(h) and kind == "s0" and n < 2):
                    pe.wait_ge(sum_taken, at - 1)
                ps = sum_ps[slot][:, :]
                if kind == "s0":
                    b, pair = n // 2, n % 2
                    if n % 2 == 0:
                        pe.wait_ge(proj_taken[b], proj_no(h, "k0") + 1)
                    for i, t in enumerate((2 * pair, 2 * pair + 1)):
                        for half in range(2):
                            c = t + half
                            for m, (x, z) in enumerate(SPLIT_PRODUCT):
                                ins = pe.matmul(ps[:, (2 * i + half) * P:(2 * i + half + 1) * P],
                                                qk[x][:, 0, b, t * P:(t + 1) * P], key_chunk(qk[z][:, 1, b, :], c),
                                                start=(m == 0), stop=(m == 2))
                else:
                    b = n
                    pe.wait_ge(proj_taken[b], proj_no(h, "k" + kind[1]) + 1)
                    for t in range(QT):
                        cols = slice(t * P, (t + 1) * P)
                        for m, (x, z) in enumerate(SPLIT_PRODUCT):
                            ins = pe.matmul(ps[:, cols], qk[x][:, 0, b, cols], qk[z][:, 1, b, cols],
                                            start=(m == 0), stop=(m == 2))
                ins.then_inc(sum_done, 1)

            def output(h, name):
                n0 = block_no(h, name)
                slot = block_slot(h, name)
                pe.wait_ge(w_split, n0 + 1)
                if name == "out0":
                    pe.wait_ge(y_split, h * 2)
                for i in range(NT):
                    k = int(name[3]) * NT + i
                    at = sum_no(h, "out", k)
                    bank_slot = sum_slot(h, "out", k)
                    pe.wait_ge(sum_taken, at - 1)
                    b, j = divmod(i, QT)
                    for m, (a, c) in enumerate(SPLIT_PRODUCT):
                        ins = pe.matmul(sum_ps[bank_slot][:, :], yT[a][:, b, j * P:(j + 1) * P],
                                        w[c][:, slot, 0:HALF], start=(m == 0), stop=(m == 2))
                    ins.then_inc(sum_done, 1)

            def between(h, name, b):
                for step in BETWEEN.get((name, b), ()):
                    if step[0] == "v2":
                        turn_values(h, 2, step[1], h - 1)
                    elif step[0] == "turn":
                        turn_probs(h, *step[1:])
                    else:
                        weigh_values(h, *step[1:])

            def head(h):
                for name in names(h):
                    if name in OUTPUTS:
                        output(h, name)
                    for b in range(NB):
                        if name in PROJ:
                            project(h, name, b)
                        if not is_first(h):
                            between(h, name, b)
                        if (name, b) in (("k2", 1), ("v2", 0)):
                            score(h, "s2", 1 - b)
                    if name == "v0":
                        for n in range(4):
                            score(h, "s0", n)
                    if name == "v1":
                        for b in range(NB):
                            score(h, "s1", b)
                    if name in ("v0", "v1"):
                        for b in range(NB):
                            turn_values(h, int(name[1]), b, h)

            head(0)
            with pe.Fori(1, A_HEADS) as h:
                head(h)
            for name in ("q0", "k0", "v0"):
                for b in range(NB):
                    between(A_HEADS, name, b)
            for name in ("out0", "out1"):
                output(A_HEADS, name)


B_HEADS = 16
B_PAIRS = B_HEADS // 2
B_NOPE, B_ROPE, B_V = 64, 32, 64
B_QK = B_NOPE + B_ROPE
B_SCALE = float(B_QK) ** -0.5
CQ, CKV = 384, 256
KQ, KKV = CQ // P, CKV // P


def stage_b_in(nc, io, X, ident, minus_half, keep):
    cT, kT, gateT = keep["cT"], keep["kT"], keep["gateT"]
    with ExitStack() as ctx:
        def sb(name, shape, dt=F32):
            return ctx.enter_context(nc.sbuf_tensor(name, shape, dt))

        def sem(name):
            return ctx.enter_context(nc.semaphore(name))

        hT = [sb(f"hTb{s}", [P, KT, NB * S], F32R) for s in "hl"]
        w = [sb(f"wb{s}", [P, KT * CQ], F32R) for s in "hl"]
        scratch = gateT[:].rearrange("p m t -> p (m t)")
        scaled_x = scratch[:, 0:QT * D].rearrange("p (j d) -> p j d", j=QT)
        latent = scratch[:, 0:NT * CQ].rearrange("p (i c) -> p i c", i=NT)
        raw = scratch[:, QT * D:QT * D + KT * CQ]
        graw = sb("graw", [P, 2, KT * P])
        g_col = sb("gb_col", [P, KT])
        gq_col = sb("gq_col", [P, KQ])
        gkv_col = sb("gkv_col", [P, KKV])
        rope_tab = sb("rope_tab", [P, 2, QT, B_ROPE // 2])
        key_rope = scratch[:, 7 * D:8 * D].rearrange("p (i c) -> p i c", i=NT)
        rot = sb("rot", [P, 4, QT, B_ROPE // 2])
        kr_raw = sb("kr_raw", [P, NT, B_ROPE])
        ss, ms, rstd = sb("ssb", [P, NT]), sb("msb", [P, NT]), sb("rstdb", [P, NT])
        stat = sb("stat", [P, 3, 2, NT])

        bank = [ctx.enter_context(nc.psum_tensor(f"bankB{i}", [P, S], F32)) for i in range(8)]
        proj_ps, turn_ps = bank[0:4], bank[4:6]

        small_loaded = sem("b_small_loaded")
        raw_loaded = sem("b_raw_loaded")
        squared = sem("b_squared")
        mean_ready = sem("b_mean_ready")
        rstd_ready = sem("b_rstd_ready")
        x_scaled = sem("b_x_scaled")
        turned = sem("b_turned")
        turn_hi = sem("b_turn_hi")
        turn_taken = sem("b_turn_taken")
        w_hi = sem("b_w_hi")
        w_split = sem("b_w_split")
        lat_done = sem("b_lat_done")
        lat_squared = sem("b_lat_squared")
        lat_mean = sem("b_lat_mean")
        lat_rstd = sem("b_lat_rstd")
        lat_taken = sem("b_lat_taken")
        zeroed = sem("b_zeroed")
        rope_step = sem("b_rope_step")
        rope_done = sem("b_rope_done")
        graw_loaded = [sem(f"b_graw_loaded{i}") for i in range(2)]
        g_hi = sem("b_g_hi")
        g_split = sem("b_g_split")
        gate_done = sem("b_gate_done")
        gate_exp = sem("b_gate_exp")
        gate_step = sem("b_gate_step")
        gate_taken = sem("b_gate_taken")

        widths = (CQ, CKV + B_ROPE)
        ktiles = (KQ, KKV)
        TQ, TKV = NORM_TURNS, NORM_TURNS + NB * KQ
        TR = TKV + NB * KKV
        gw = [t[:, 0:2 * KT * P].rearrange("p (s c) -> p s c", s=2) for t in w]

        block = ctx.enter_context(nc.Block())

        @block.sync
        def _(sp):
            for dst, name in ((g_col, "g1"), (gq_col, "gq"), (gkv_col, "gkv")):
                sp.dma_start(dst[:, :], io[name]).then_inc(small_loaded, 16)
            sp.dma_start(rope_tab[:].rearrange("p a j c -> p (a j c)"), io["rope_tok"]).then_inc(small_loaded, 16)
            sp.dma_start(raw[:, :], io["b_w_cq"]).then_inc(raw_loaded, 16)
            for n in range(2):
                sp.dma_start(graw[:, n, :], io["b_w_gate"][n]).then_inc(graw_loaded[n], 16)
            sp.wait_ge(w_split, KT)
            sp.dma_start(raw[:, 0:KT * widths[1]], io["b_w_ckv"]).then_inc(raw_loaded, 16)
            for n in range(2, KT):
                sp.wait_ge(g_split, n - 1)
                sp.dma_start(graw[:, n % 2, :], io["b_w_gate"][n]).then_inc(graw_loaded[n % 2], 16)

        @block.gpsimd
        def _(pool):
            pool.memset(key_rope, 0.0).then_inc(zeroed, 1)
            pool.wait_ge(zeroed, 1)
            pool.wait_ge(mean_ready, 1)
            pool.tensor_tensor(rstd[:, :], ms[:, :], minus_half[:, :], ALU.pow).then_inc(rstd_ready, 1)
            for n in range(2 * NT):
                c, i = divmod(n, NT)
                pool.wait_ge(lat_mean, n + 1)
                pool.tensor_tensor(stat[:, 2, c, i:i + 1], stat[:, 1, c, i:i + 1], minus_half[:, 0:1],
                                   ALU.pow).then_inc(lat_rstd, 1)

        @block.scalar
        def _(act):
            for i in range(NT):
                act.activation(hT[i % 2][:, i // 2, :], X[:, i, :], ACT.Square,
                               accum_out=ss[:, i:i + 1]).then_inc(squared, 1)

            def split_w(c, k):
                act.wait_ge(raw_loaded, 16 * (c + 1))
                cols = slice(k * widths[c], (k + 1) * widths[c])
                act.activation(w[HI][:, cols], raw[:, cols], ACT.Copy).then_inc(w_hi, 1)

            def turn(n, dst, scale=None):
                act.wait_ge(turned, n + 1)
                if scale is None:
                    act.activation(dst, turn_ps[n % 2][:, :], ACT.Copy).then_inc(turn_hi, 1)
                else:
                    act.activation(dst, turn_ps[n % 2][:, :], ACT.Copy, scale=scale).then_inc(turn_hi, 1)

            for k in range(KT):
                split_w(0, k)
            act.wait_ge(small_loaded, 64)
            for b in range(NB):
                for k in range(KT):
                    turn(b * KT + k, hT[HI][:, k, b * S:(b + 1) * S], g_col[:, k:k + 1])

            def latents(c):
                for i in range(NT):
                    n = c * NT + i
                    act.wait_ge(lat_done, n + 1)
                    ps = proj_ps[n % 4]
                    cols = CQ if c == 0 else CKV
                    act.activation(latent[:, i, 0:cols], ps[:, 0:cols], ACT.Square,
                                   accum_out=stat[:, 0, c, i:i + 1]).then_inc(lat_squared, 1)
                    if c == 0 and i == NT - 1:
                        for k in range(KT):
                            split_w(1, k)
                    if i % QT == QT - 1 and i == NT - 1:
                        for b in range(NB):
                            for k in range(ktiles[c]):
                                turn((TQ, TKV)[c] + b * ktiles[c] + k,
                                     cT[c][HI][:, k, b * S:(b + 1) * S], (gq_col, gkv_col)[c][:, k:k + 1])

            latents(0)
            latents(1)
            for b in range(NB):
                n = TR + b
                act.wait_ge(turned, n + 1)
                for par in range(2):
                    ins = act.activation(kT[HI][B_NOPE:B_QK, par, b, :], turn_ps[n % 2][B_NOPE:B_QK, :], ACT.Copy)
                ins.then_inc(turn_hi, 1)

            def split_gate(n):
                act.wait_ge(graw_loaded[n % 2], 16 * (n // 2 + 1))
                if n < 2:
                    act.wait_ge(lat_done, 2 * NT)
                else:
                    act.wait_ge(gate_done, 2 * (n - 1))
                act.activation(gw[HI][:, n % 2, :], graw[:, n % 2, :], ACT.Copy).then_inc(g_hi, 1)

            split_gate(0)
            split_gate(1)
            act.wait_ge(turned, TR + NB)
            for n in range(KT):
                for b in range(NB):
                    act.wait_ge(gate_done, 2 * n + b + 1)
                    act.activation(gateT[:, n, b * S:(b + 1) * S], proj_ps[(2 * n + b) % 4][:, :], ACT.Exp,
                                   scale=-1.0).then_inc(gate_exp, 1)
                if n + 2 < KT:
                    split_gate(n + 2)

        @block.vector
        def _(dve):
            dve.wait_ge(squared, NT)
            dve.tensor_scalar(ms[:, :], ss[:, :], 1.0 / D, RMS_EPS, ALU.mult, ALU.add).then_inc(mean_ready, 1)
            dve.wait_ge(rstd_ready, 1)

            def split_w(c, k):
                cols = slice(k * widths[c], (k + 1) * widths[c])
                dve.wait_ge(w_hi, c * KT + k + 1)
                dve.tensor_tensor(w[LO][:, cols], raw[:, cols], w[HI][:, cols], ALU.subtract).then_inc(w_split, 1)

            def turn(n, hi, lo, scale):
                dve.wait_ge(turn_hi, n + 1)
                dve.scalar_tensor_tensor(lo, turn_ps[n % 2][:, :], scale, hi, ALU.mult,
                                         ALU.subtract).then_inc(turn_taken, 1)

            for b in range(NB):
                if b:
                    dve.wait_ge(turned, KT * b)
                for j in range(QT):
                    i = b * QT + j
                    ins = dve.tensor_scalar(scaled_x[:, j, :], X[:, i, :], rstd[:, i:i + 1], None, ALU.mult)
                ins.then_inc(x_scaled, 1)
                for k in range(KT):
                    if b == 0:
                        split_w(0, k)
                if b == 0:
                    dve.wait_ge(small_loaded, 64)
                for k in range(KT):
                    cols = slice(b * S, (b + 1) * S)
                    turn(b * KT + k, hT[HI][:, k, cols], hT[LO][:, k, cols], g_col[:, k:k + 1])

            for c in range(2):
                cols = (CQ, CKV)[c]
                for i in range(NT):
                    n = c * NT + i
                    dve.wait_ge(lat_squared, n + 1)
                    dve.tensor_scalar(stat[:, 1, c, i:i + 1], stat[:, 0, c, i:i + 1], 1.0 / cols, RMS_EPS,
                                      ALU.mult, ALU.add).then_inc(lat_mean, 1)
                    if c == 1:
                        dve.tensor_copy(kr_raw[:, i, :], proj_ps[n % 4][:, CKV:CKV + B_ROPE])
                    dve.wait_ge(lat_rstd, n + 1)
                    dve.tensor_scalar(latent[:, i, 0:cols], proj_ps[n % 4][:, 0:cols], stat[:, 2, c, i:i + 1],
                                      None, ALU.mult).then_inc(lat_taken, 1)
                if c == 0:
                    for k in range(KT):
                        split_w(1, k)
                for b in range(NB):
                    for k in range(ktiles[c]):
                        tok = slice(b * S, (b + 1) * S)
                        turn((TQ, TKV)[c] + b * ktiles[c] + k, cT[c][HI][:, k, tok], cT[c][LO][:, k, tok],
                             (gq_col, gkv_col)[c][:, k:k + 1])
            dve.wait_ge(lat_taken, 2 * NT)
            dve.wait_ge(zeroed, 1)
            half = B_ROPE // 2
            for b in range(NB):
                x1 = kr_raw[:, b * QT:(b + 1) * QT, 0:half]
                x2 = kr_raw[:, b * QT:(b + 1) * QT, half:B_ROPE]
                cos, sin = rope_tab[:, 0], rope_tab[:, 1]
                if b:
                    dve.wait_ge(rope_done, b)
                for m, (x, tab) in enumerate(((x1, cos), (x2, sin), (x1, sin), (x2, cos))):
                    ins = dve.tensor_tensor(rot[:, m], x, tab, ALU.mult)
                ins.then_inc(rope_step, 1)
                dve.wait_ge(rope_step, b + 1)
                dst = key_rope[:, b * QT:(b + 1) * QT]
                dve.tensor_tensor(dst[:, :, B_NOPE:B_NOPE + half], rot[:, 0], rot[:, 1], ALU.subtract)
                dve.tensor_tensor(dst[:, :, B_NOPE + half:B_QK], rot[:, 2], rot[:, 3], ALU.add).then_inc(rope_done, 1)
            for b in range(NB):
                n = TR + b
                dve.wait_ge(turn_hi, n + 1)
                for par in range(2):
                    ins = dve.tensor_tensor(kT[LO][B_NOPE:B_QK, par, b, :], turn_ps[n % 2][B_NOPE:B_QK, :],
                                            kT[HI][B_NOPE:B_QK, par, b, :], ALU.subtract)
                ins.then_inc(turn_taken, 1)

            def split_gate(n):
                dve.wait_ge(g_hi, n + 1)
                dve.tensor_tensor(gw[LO][:, n % 2, :], graw[:, n % 2, :], gw[HI][:, n % 2, :],
                                  ALU.subtract).then_inc(g_split, 1)

            split_gate(0)
            split_gate(1)
            for n in range(KT):
                for b in range(NB):
                    m = 2 * n + b
                    g = gateT[:, n, b * S:(b + 1) * S]
                    dve.wait_ge(gate_exp, m + 1)
                    dve.tensor_scalar(g, g, 1.0, None, ALU.add).then_inc(gate_step, 1)
                    dve.wait_ge(gate_step, 2 * m + 1)
                    dve.reciprocal(g, g).then_inc(gate_step, 1)
                    dve.wait_ge(gate_step, 2 * m + 2)
                    dve.tensor_tensor(g, proj_ps[m % 4][:, :], g, ALU.mult).then_inc(gate_taken, 1)
                if n + 2 < KT:
                    split_gate(n + 2)

        @block.tensor
        def _(pe):
            def turn(n, tiles):
                if n >= 2:
                    pe.wait_ge(turn_taken, n - 1)
                for j, tile in enumerate(tiles):
                    ins = pe.transpose(turn_ps[n % 2][:, j * P:(j + 1) * P], tile, ident[:, :])
                ins.then_inc(turned, 1)

            for b in range(NB):
                pe.wait_ge(x_scaled, b + 1)
                for k in range(KT):
                    turn(b * KT + k, [scaled_x[:, j, k * P:(k + 1) * P] for j in range(QT)])

            for c in range(2):
                for i in range(NT):
                    n = c * NT + i
                    if n >= 4:
                        pe.wait_ge(lat_taken, n - 3)
                    if c == 0:
                        pe.wait_ge(turn_taken, (i // QT + 1) * KT)
                    for k in range(KT):
                        pe.wait_ge(w_split, c * KT + k + 1)
                        for m, (a, z) in enumerate(SPLIT_PRODUCT):
                            ins = pe.matmul(proj_ps[n % 4][:, 0:widths[c]], hT[a][:, k, i * P:(i + 1) * P],
                                            w[z][:, k * widths[c]:(k + 1) * widths[c]],
                                            start=(k == 0 and m == 0), stop=(k == KT - 1 and m == 2))
                    ins.then_inc(lat_done, 1)
                for b in range(NB):
                    pe.wait_ge(lat_taken, c * NT + (b + 1) * QT)
                    for k in range(ktiles[c]):
                        turn((TQ, TKV)[c] + b * ktiles[c] + k,
                             [latent[:, b * QT + j, k * P:(k + 1) * P] for j in range(QT)])
            for b in range(NB):
                pe.wait_ge(rope_done, b + 1)
                turn(TR + b, [key_rope[:, b * QT + j, :] for j in range(QT)])
            for n in range(KT):
                pe.wait_ge(g_split, n + 1)
                for b in range(NB):
                    m = 2 * n + b
                    if m >= 4:
                        pe.wait_ge(gate_taken, m - 3)
                    for k in range(KT):
                        for q, (a, z) in enumerate(SPLIT_PRODUCT):
                            ins = pe.matmul(proj_ps[m % 4][:, :], gw[a][:, n % 2, k * P:(k + 1) * P],
                                            hT[z][:, k, b * S:(b + 1) * S], start=(k == 0 and q == 0),
                                            stop=(k == KT - 1 and q == 2))
                    ins.then_inc(gate_done, 1)


UNITS = ((0, 0), (0, 1), (1, 0), (1, 1))


def steps_b(prev, nxt):
    def attend(u, scored, extras):
        fill = [[("score", scored, t)] + ([("norm", scored, t - 1)] if t else []) for t in range(QT)]
        if u is None:
            out = [[f] for f in fill]
        else:
            out = [[[("turn", u, 0), ("turn", u, 1)], fill[0]],
                   [[("weigh", u, 0), ("turn", u, 2)], fill[1]],
                   [[("weigh", u, 1), ("turn", u, 3)], fill[2]],
                   [[("weigh", u, 2)], fill[3], [("weigh", u, 3)]]]
        steps = []
        for n, parts in enumerate(out):
            for part in parts:
                steps += part
            steps += [e for at, e in extras if at == n]
        return steps + [("norm", scored, QT - 1)]

    old = [("fold", -2)] if prev else []
    s = [("q_up", 0, 0)] + old + [("q_up", 0, 1), ("k_up", 0), ("rope", 0, 0)]
    s += [("y", -2)] if prev else []
    s += [("k_up", 1), ("rope", 0, 1)]
    s += attend(-1 if prev else None, 0, [])
    s += [("v_up", 0)] + ([("fold", -1)] if prev else []) + [("v_up", 1), ("q_up", 1, 0), ("v_turn", 0)]
    s += [("q_up", 1, 1)] + ([("y", -1)] if prev else []) + [("v_turn", 1), ("rope", 1, 0)]
    s += attend(0, 1, [(0, ("rope", 1, 1))] + ([(1, ("split_kv",)), (2, ("split_q",))] if nxt else []))
    s += [("out", 0)] if prev else []
    s += [("fold", 0)] + [("out", n) for n in range(1, 8) if prev]
    s += attend(1, 2, [(1, ("split_out", 0))])
    s += [("out", 8)] if prev else []
    s += [("fold", 1)] + [("out", n) for n in range(9, 16) if prev]
    s += attend(2, 3, [(0, ("y", 0)), (1, ("split_out", 1)), (2, ("y", 1))])
    return s


LAST_STEPS = [("fold", -2), ("turn", -1, 0), ("turn", -1, 1), ("y", -2), ("weigh", -1, 0), ("turn", -1, 2),
              ("weigh", -1, 1), ("turn", -1, 3), ("weigh", -1, 2), ("weigh", -1, 3), ("fold", -1),
              ("y", -1)] + [("out", n) for n in range(2 * NT)]
RING = 5
USERS = ("k_up", "q_up", "v_up", "score", "out")
TURNERS = ("turn", "v_turn")


def places(banks, kinds):
    first, each, last = ([s for s in steps if s[0] in kinds]
                         for steps in (steps_b(False, True), steps_b(True, True), LAST_STEPS))
    assert len(each) % banks == 0

    def place(p, step):
        if isinstance(p, int) and p == 0:
            n = first.index(step)
            return n, n % banks, n // banks
        n = (last if isinstance(p, int) and p == B_PAIRS else each).index(step)
        slot = n % banks
        before = len(range(slot, len(first), banks)) - len(each) // banks + n // banks
        return p * len(each) + (len(first) - len(each) + n), slot, p * (len(each) // banks) + before
    return place


ring = places(RING, USERS)
turning = places(2, TURNERS)


def stage_b_heads(nc, io, X, ident, keep):
    cT, kT, gateT = keep["cT"], keep["kT"], keep["gateT"]
    with ExitStack() as ctx:
        def sb(name, shape, dt=F32):
            return ctx.enter_context(nc.sbuf_tensor(name, shape, dt))

        def sem(name):
            return ctx.enter_context(nc.semaphore(name))

        qT = [sb(f"qT{s}", [P, 2, NB, S], F32R) for s in "hl"]
        v = sb("v", [P, NB, QT, 2, 2 * B_V], F32R)
        vT = sb("vTb", [P, NB, S])
        prob = sb("probb", [P, 2, QT, S])
        pT = [sb(f"pTb{s}", [P, 2, S], F32R) for s in "hl"]
        o_low = sb("o_low", [P, S])
        y = sb("yb", [P, NB, S])
        yT = [sb(f"yTb{s}", [P, NB, S], F32R) for s in "hl"]
        rope = sb("rope", [P, 2, 2, S])
        table = sb("table", [P, S])
        raw_q, raw_kv, raw_o = sb("raw_q", [P, KQ * 2 * P]), sb("raw_kv", [P, KKV * 2 * P]), sb("raw_o", [P, HALF])
        wq = [sb(f"wq{s}", [P, KQ * 2 * P], F32R) for s in "hl"]
        wkv = [sb(f"wkv{s}", [P, KKV * 2 * P], F32R) for s in "hl"]
        wo = [sb(f"wo{s}", [P, D], F32R) for s in "hl"]
        negmax = sb("negmaxb", [P, 4, QT])
        total = sb("total", [P, 4, QT])
        inv = sb("inv", [P, 4, QT])

        bank = [ctx.enter_context(nc.psum_tensor(f"bankC{i}", [P, S], F32)) for i in range(8)]
        ring_ps, turn_ps, o_ps = bank[0:RING], bank[5:7], bank[7]

        table_loaded = sem("table_loaded")
        q_loaded, kv_loaded, o_loaded = sem("q_loaded"), sem("kv_loaded"), sem("o_loaded")
        q_w_hi, kv_w_hi, o_w_hi = sem("q_w_hi"), sem("kv_w_hi"), sem("o_w_hi")
        q_w_split, kv_w_split, o_w_split = sem("q_w_split"), sem("kv_w_split"), sem("o_w_split")
        ring_done = sem("ring_done")
        ring_taken = [sem(f"ring_taken{i}") for i in range(RING)]
        k_hi, k_split, q_hi, v_copied = sem("k_hi"), sem("k_split"), sem("q_hi"), sem("v_copied")
        rope_parts, rope_sum, rope_hi, rope_split = sem("rope_parts"), sem("rope_sum"), sem("rope_hi"), sem("rope_split")
        negmax_ready, inv_ready, prob_ready = sem("negmaxb_ready"), sem("inv_ready"), sem("probb_ready")
        turned, turn_hi, turn_taken = sem("turnedb"), sem("turnb_hi"), sem("turnb_taken")
        o_done, o_copied, o_taken = sem("ob_done"), sem("o_copied"), sem("o_taken")
        y_ready, y_hi, y_split = sem("yb_ready"), sem("yb_hi"), sem("yb_split")

        def unit(p, u):
            return p * 4 + u

        def run(body):
            def go(eng):
                body(0, steps_b(False, True))
                with eng.Fori(1, B_PAIRS - 1) as p:
                    body(p, steps_b(True, True))
                body(B_PAIRS - 1, steps_b(True, False))
                body(B_PAIRS, LAST_STEPS)
            return go

        block = ctx.enter_context(nc.Block())

        @block.sync
        def _(sp):
            def load_q(p):
                sp.dma_start(raw_q[:, :], io["b_w_q"][bass.ds(p, 1)].rearrange("o p c -> (o p) c")).then_inc(q_loaded, 16)

            def load_kv(p):
                sp.dma_start(raw_kv[:, :], io["b_w_kv"][bass.ds(p, 1)].rearrange("o p c -> (o p) c")).then_inc(kv_loaded, 16)

            load_kv(0)
            load_q(0)
            sp.dma_start(table[:, :], io["rope_dim"]).then_inc(table_loaded, 16)

            def body(p, steps):
                for s in steps:
                    if s == ("q_up", 0, 0) and ("split_kv",) in steps:
                        sp.wait_ge(kv_w_split, p + 1)
                        load_kv(p + 1)
                        sp.wait_ge(q_w_split, p + 1)
                        load_q(p + 1)
                    if s[0] == "split_out":
                        half = s[1]
                        if not (isinstance(p, int) and p == 0 and half == 0):
                            sp.wait_ge(o_w_split, 2 * p + half)
                        src = io["b_w_out"][bass.ds(p, 1), :, half * HALF:(half + 1) * HALF]
                        sp.dma_start(raw_o[:, :], src.rearrange("o p c -> (o p) c")).then_inc(o_loaded, 16)

            run(body)(sp)

        @block.gpsimd
        def _(pool):
            def split(w, raw, hi, ready, n, cols):
                pool.wait_ge(hi, n)
                pool.tensor_tensor(w[LO][:, cols], raw, w[HI][:, cols], ALU.subtract).then_inc(ready, 1)
                pool.wait_ge(ready, n)

            split(wkv, raw_kv[:, :], kv_w_hi, kv_w_split, 1, slice(0, KKV * 2 * P))
            split(wq, raw_q[:, :], q_w_hi, q_w_split, 1, slice(0, KQ * 2 * P))

            def body(p, steps):
                for s in steps:
                    if s[0] == "split_kv":
                        split(wkv, raw_kv[:, :], kv_w_hi, kv_w_split, p + 2, slice(0, KKV * 2 * P))
                    elif s[0] == "split_q":
                        split(wq, raw_q[:, :], q_w_hi, q_w_split, p + 2, slice(0, KQ * 2 * P))
                    elif s[0] == "split_out":
                        split(wo, raw_o[:, :], o_w_hi, o_w_split, 2 * p + s[1] + 1,
                              slice(s[1] * HALF, (s[1] + 1) * HALF))
                    elif s[0] == "q_up":
                        hd, b = s[1:]
                        n = unit(p, 2 * hd + b)
                        part = rope[B_NOPE:B_QK, b]
                        pool.wait_ge(rope_parts, n + 1)
                        pool.tensor_tensor(part[:, 0], part[:, 0], part[:, 1], ALU.add).then_inc(rope_sum, 1)
                    elif s[0] == "rope":
                        hd, b = s[1:]
                        n = unit(p, 2 * hd + b)
                        rows = slice(B_NOPE, B_QK)
                        pool.wait_ge(rope_hi, n + 1)
                        pool.tensor_tensor(qT[LO][rows, hd, b, :], rope[rows, b, 0, :], qT[HI][rows, hd, b, :],
                                           ALU.subtract).then_inc(rope_split, 1)
                        pool.wait_ge(rope_split, n + 1)
                    elif s[0] == "norm":
                        u, t = s[1:]
                        n = unit(p, u) * QT + t
                        tile = prob[:, u % 2, t, :]
                        pool.wait_ge(inv_ready, n + 1)
                        pool.tensor_tensor(tile, tile, inv[:, u, t:t + 1].to_broadcast([P, S]),
                                           ALU.mult).then_inc(prob_ready, 1)
                        pool.wait_ge(prob_ready, n + 1)
                    elif s[0] == "fold":
                        n = unit(p, s[1])
                        hd, b = UNITS[s[1] % 4]
                        rows = slice(hd * B_V, (hd + 1) * B_V)
                        pair = p - 1 if s[1] < 0 else p
                        g = gateT[rows, bass.ds(pair, 1), b * S:(b + 1) * S].rearrange("p o t -> p (o t)")
                        pool.wait_ge(o_taken, n + 1)
                        pool.tensor_tensor(y[rows, b, :], y[rows, b, :], g, ALU.mult).then_inc(y_ready, 1)
                        pool.wait_ge(y_ready, n + 1)
                    elif s[0] == "y":
                        n = unit(p, s[1])
                        hd, b = UNITS[s[1] % 4]
                        rows = slice(hd * B_V, (hd + 1) * B_V)
                        pool.wait_ge(y_hi, n + 1)
                        pool.tensor_tensor(yT[LO][rows, b, :], y[rows, b, :], yT[HI][rows, b, :],
                                           ALU.subtract).then_inc(y_split, 1)
                        pool.wait_ge(y_split, n + 1)

            run(body)(pool)

        @block.scalar
        def _(act):
            def split(w, raw, loaded, hi, n, cols):
                act.wait_ge(loaded, n * 16)
                act.activation(w[HI][:, cols], raw, ACT.Copy).then_inc(hi, 1)

            split(wkv, raw_kv[:, :], kv_loaded, kv_w_hi, 1, slice(0, KKV * 2 * P))
            split(wq, raw_q[:, :], q_loaded, q_w_hi, 1, slice(0, KQ * 2 * P))

            def body(p, steps):
                for s in steps:
                    if s[0] in USERS:
                        n, slot, _ = ring(p, s)
                        ps = ring_ps[slot]
                    if s[0] == "split_kv":
                        act.wait_ge(ring_done, ring(p, ("v_up", 1))[0] + 1)
                        split(wkv, raw_kv[:, :], kv_loaded, kv_w_hi, p + 2, slice(0, KKV * 2 * P))
                    elif s[0] == "split_q":
                        act.wait_ge(ring_done, ring(p, ("q_up", 1, 1))[0] + 1)
                        split(wq, raw_q[:, :], q_loaded, q_w_hi, p + 2, slice(0, KQ * 2 * P))
                    elif s[0] == "split_out":
                        if not (isinstance(p, int) and p == 0):
                            act.wait_ge(ring_done, ring(p, ("out", (s[1] + 1) * NT - 1))[0] + 1)
                        split(wo, raw_o[:, :], o_loaded, o_w_hi, 2 * p + s[1] + 1,
                              slice(s[1] * HALF, (s[1] + 1) * HALF))
                    elif s[0] == "k_up":
                        act.wait_ge(ring_done, n + 1)
                        for hd in range(2):
                            ins = act.activation(kT[HI][0:B_NOPE, hd, s[1], :],
                                                 ps[hd * B_NOPE:(hd + 1) * B_NOPE, :], ACT.Copy)
                        ins.then_inc(k_hi, 1)
                    elif s[0] == "q_up":
                        hd, b = s[1:]
                        act.wait_ge(ring_done, n + 1)
                        act.activation(qT[HI][0:B_NOPE, hd, b, :], ps[0:B_NOPE, :], ACT.Copy,
                                       scale=B_SCALE).then_inc(q_hi, 1)
                    elif s[0] == "rope":
                        hd, b = s[1:]
                        act.wait_ge(rope_sum, unit(p, 2 * hd + b) + 1)
                        act.activation(qT[HI][B_NOPE:B_QK, hd, b, :], rope[B_NOPE:B_QK, b, 0, :],
                                       ACT.Copy).then_inc(rope_hi, 1)
                    elif s[0] == "v_up":
                        b = s[1]
                        act.wait_ge(ring_done, n + 1)
                        act.activation(vT[:, b, :], ps[:, :], ACT.Copy).then_inc(ring_taken[slot], 1)
                    elif s[0] == "v_turn":
                        b = s[1]
                        n, bank, _ = turning(p, s)
                        act.wait_ge(turned, n + 1)
                        act.activation(v[:, b, :, :, 0:B_V].rearrange("p t h c -> p (t h) c"),
                                       turn_ps[bank][:].rearrange("p (a c) -> p a c", c=B_V),
                                       ACT.Copy).then_inc(turn_hi, 1)
                    elif s[0] == "score":
                        u, t = s[1:]
                        act.wait_ge(negmax_ready, unit(p, u) * QT + t + 1)
                        act.activation(prob[:, u % 2, t, :], ps[:, :], ACT.Exp, bias=negmax[:, u, t:t + 1],
                                       accum_out=total[:, u, t:t + 1]).then_inc(ring_taken[slot], 1)
                    elif s[0] == "turn":
                        u, kb = s[1:]
                        act.wait_ge(turned, turning(p, s)[0] + 1)
                        act.activation(pT[HI][:, kb % 2, :], turn_ps[turning(p, s)[1]][:, :], ACT.Copy).then_inc(turn_hi, 1)
                    elif s[0] == "fold":
                        N = unit(p, s[1])
                        hd, b = UNITS[s[1] % 4]
                        rows = slice(hd * B_V, (hd + 1) * B_V)
                        act.wait_ge(o_done, N + 1)
                        act.activation(o_low[0:B_V, :], o_ps[B_V:2 * B_V, :], ACT.Copy).then_inc(o_copied, 1)
                    elif s[0] == "y":
                        N = unit(p, s[1])
                        hd, b = UNITS[s[1] % 4]
                        rows = slice(hd * B_V, (hd + 1) * B_V)
                        act.wait_ge(y_ready, N + 1)
                        act.activation(yT[HI][rows, b, :], y[rows, b, :], ACT.Copy).then_inc(y_hi, 1)

            run(body)(act)

        @block.vector
        def _(dve):
            dve.wait_ge(table_loaded, 16)

            def body(p, steps):
                for s in steps:
                    if s[0] in USERS:
                        n, slot, used = ring(p, s)
                        ps = ring_ps[slot]
                    if s[0] == "k_up":
                        b = s[1]
                        dve.wait_ge(k_hi, p * 2 + b + 1)
                        dve.tensor_tensor(kT[LO][0:B_NOPE, 0, b, :], ps[0:B_NOPE, :], kT[HI][0:B_NOPE, 0, b, :],
                                          ALU.subtract).then_inc(k_split, 1)
                        dve.tensor_tensor(kT[LO][0:B_NOPE, 1, b, :], ps[B_NOPE:2 * B_NOPE, :],
                                          kT[HI][0:B_NOPE, 1, b, :], ALU.subtract).then_inc(ring_taken[slot], 1)
                    elif s[0] == "q_up":
                        hd, b = s[1:]
                        N = unit(p, 2 * hd + b)
                        dve.wait_ge(ring_done, n + 1)
                        if not (isinstance(p, int) and p == 0 and hd == 0):
                            dve.wait_ge(rope_split, N - 1)
                        dve.tensor_tensor(rope[B_NOPE:B_QK, b, 0, :], ps[B_NOPE:B_QK, :], table[B_NOPE:B_QK, :], ALU.mult)
                        dve.tensor_tensor(rope[B_NOPE:B_QK, b, 1, :], ps[B_QK:P, :], table[B_QK:P, :],
                                          ALU.mult).then_inc(rope_parts, 1)
                        dve.wait_ge(q_hi, N + 1)
                        dve.scalar_tensor_tensor(qT[LO][0:B_NOPE, hd, b, :], ps[0:B_NOPE, :], B_SCALE,
                                                 qT[HI][0:B_NOPE, hd, b, :], ALU.mult,
                                                 ALU.subtract).then_inc(ring_taken[slot], 1)
                    elif s[0] == "v_turn":
                        b = s[1]
                        n, bank, _ = turning(p, s)
                        dve.wait_ge(turn_hi, n + 1)
                        dve.tensor_tensor(v[:, b, :, :, B_V:2 * B_V].rearrange("p t h c -> p (t h) c"),
                                          turn_ps[bank][:].rearrange("p (a c) -> p a c", c=B_V),
                                          v[:, b, :, :, 0:B_V].rearrange("p t h c -> p (t h) c"),
                                          ALU.subtract).then_inc(turn_taken, 1)
                    elif s[0] == "score":
                        u, t = s[1:]
                        dve.wait_ge(ring_done, n + 1)
                        dve.tensor_reduce(negmax[:, u, t:t + 1], ps[:, :], AX.X, ALU.max,
                                          negate=True).then_inc(negmax_ready, 1)
                    elif s[0] == "norm":
                        u, t = s[1:]
                        _, slot, used = ring(p, ("score", u, t))
                        dve.wait_ge(ring_taken[slot], used + 1)
                        dve.reciprocal(inv[:, u, t:t + 1], total[:, u, t:t + 1]).then_inc(inv_ready, 1)
                    elif s[0] == "turn":
                        u, kb = s[1:]
                        dve.wait_ge(turn_hi, turning(p, s)[0] + 1)
                        dve.tensor_tensor(pT[LO][:, kb % 2, :], turn_ps[turning(p, s)[1]][:, :], pT[HI][:, kb % 2, :],
                                          ALU.subtract).then_inc(turn_taken, 1)
                    elif s[0] == "fold":
                        N = unit(p, s[1])
                        hd, b = UNITS[s[1] % 4]
                        rows = slice(hd * B_V, (hd + 1) * B_V)
                        dve.wait_ge(o_copied, N + 1)
                        dve.tensor_tensor(y[rows, b, :], o_ps[0:B_V, :], o_low[0:B_V, :], ALU.add).then_inc(o_taken, 1)
                    elif s[0] == "out":
                        half, i = divmod(s[1], NT)
                        cols = slice(half * HALF, (half + 1) * HALF)
                        dve.wait_ge(ring_done, n + 1)
                        dve.tensor_tensor(X[:, i, cols], ps[:, :], X[:, i, cols], ALU.add).then_inc(ring_taken[slot], 1)

            run(body)(dve)

        @block.tensor
        def _(pe):
            def free_turning(p, s):
                n, _, used = turning(p, s)
                if not (isinstance(p, int) and p == 0 and used == 0):
                    pe.wait_ge(turn_taken, n - 1)

            def body(p, steps):
                first = isinstance(p, int) and p == 0
                for s in steps:
                    if s[0] in USERS:
                        n, slot, used = ring(p, s)
                        ps = ring_ps[slot]
                        if not (first and used == 0):
                            pe.wait_ge(ring_taken[slot], used)
                    if s[0] == "k_up":
                        b = s[1]
                        pe.wait_ge(kv_w_split, p + 1)
                        for k in range(KKV):
                            for m, (a, z) in enumerate(SPLIT_PRODUCT):
                                ins = pe.matmul(ps[:, :], wkv[a][:, k * 2 * P:k * 2 * P + P],
                                                cT[1][z][:, k, b * S:(b + 1) * S],
                                                start=(k == 0 and m == 0), stop=(k == KKV - 1 and m == 2))
                        ins.then_inc(ring_done, 1)
                    elif s[0] == "q_up":
                        hd, b = s[1:]
                        pe.wait_ge(q_w_split, p + 1)
                        for k in range(KQ):
                            for m, (a, z) in enumerate(SPLIT_PRODUCT):
                                ins = pe.matmul(ps[:, :], wq[a][:, (2 * k + hd) * P:(2 * k + hd + 1) * P],
                                                cT[0][z][:, k, b * S:(b + 1) * S],
                                                start=(k == 0 and m == 0), stop=(k == KQ - 1 and m == 2))
                        ins.then_inc(ring_done, 1)
                    elif s[0] == "v_up":
                        b = s[1]
                        for k in range(KKV):
                            for m, (a, z) in enumerate(SPLIT_PRODUCT):
                                ins = pe.matmul(ps[:, :], wkv[a][:, k * 2 * P + P:(k + 1) * 2 * P],
                                                cT[1][z][:, k, b * S:(b + 1) * S],
                                                start=(k == 0 and m == 0), stop=(k == KKV - 1 and m == 2))
                        ins.then_inc(ring_done, 1)
                    elif s[0] == "score":
                        u, t = s[1:]
                        hd, b = UNITS[u]
                        if t == 0:
                            pe.wait_ge(rope_split, unit(p, u) + 1)
                        for m, (a, z) in enumerate(SPLIT_PRODUCT):
                            if t == 0 and z == LO:
                                _, k_slot, k_used = ring(p, ("k_up", b))
                                pe.wait_ge(ring_taken[k_slot], k_used + 1)
                            if t == 0 and a == LO:
                                _, q_slot, q_used = ring(p, ("q_up", hd, b))
                                pe.wait_ge(ring_taken[q_slot], q_used + 1)
                            ins = pe.matmul(ps[:, :], qT[a][0:B_QK, hd, b, t * P:(t + 1) * P], kT[z][0:B_QK, hd, b, :],
                                            start=(m == 0), stop=(m == 2))
                        ins.then_inc(ring_done, 1)
                    elif s[0] == "turn":
                        u, kb = s[1:]
                        free_turning(p, s)
                        if kb == 0:
                            pe.wait_ge(prob_ready, (unit(p, u) + 1) * QT)
                        bank = turning(p, s)[1]
                        for t in range(QT):
                            ins = pe.transpose(turn_ps[bank][:, t * P:(t + 1) * P],
                                               prob[:, u % 2, t, kb * P:(kb + 1) * P], ident[:, :])
                        ins.then_inc(turned, 1)
                    elif s[0] == "v_turn":
                        b = s[1]
                        free_turning(p, s)
                        _, slot, used = ring(p, ("v_up", b))
                        pe.wait_ge(ring_taken[slot], used + 1)
                        bank = turning(p, s)[1]
                        for t in range(QT):
                            ins = pe.transpose(turn_ps[bank][:, t * P:(t + 1) * P], vT[:, b, t * P:(t + 1) * P],
                                               ident[:, :])
                        ins.then_inc(turned, 1)
                    elif s[0] == "weigh":
                        u, kb = s[1:]
                        N = unit(p, u)
                        hd, b = UNITS[u % 4]
                        pe.wait_ge(turn_taken, turning(p, ("turn", u, kb))[0] + 1)
                        if kb == 0 and not (first and u == 0):
                            pe.wait_ge(o_taken, N)
                        for part in (HI, LO):
                            ins = pe.matmul(o_ps[:, :], v[:, b, kb, hd, :], pT[part][:, kb % 2, :],
                                            start=(kb == 0 and part == HI), stop=(kb == 3 and part == LO))
                        if kb == 3:
                            ins.then_inc(o_done, 1)
                    elif s[0] == "out":
                        half, i = divmod(s[1], NT)
                        b, j = divmod(i, QT)
                        if s[1] == 0:
                            pe.wait_ge(y_split, unit(p, 0))
                        if i == 0:
                            pe.wait_ge(o_w_split, 2 * p - 1 + half)
                        for m, (a, z) in enumerate(SPLIT_PRODUCT):
                            ins = pe.matmul(ps[:, :], yT[a][:, b, j * P:(j + 1) * P],
                                            wo[z][:, half * HALF:(half + 1) * HALF], start=(m == 0), stop=(m == 2))
                        ins.then_inc(ring_done, 1)

            run(body)(pe)


def stage_final(nc, io, X, minus_half):
    with ExitStack() as ctx:
        def sb(name, shape, dt=F32):
            return ctx.enter_context(nc.sbuf_tensor(name, shape, dt))

        def sem(name):
            return ctx.enter_context(nc.semaphore(name))

        junk = sb("junk", [P, NT, D])
        out = sb("out", [P, NT, D])
        g_row = sb("g_row", [P, D])
        ss, ms, rstd = sb("ssf", [P, NT]), sb("msf", [P, NT]), sb("rstdf", [P, NT])
        g_loaded, squared, mean_ready = sem("f_g_loaded"), sem("f_squared"), sem("f_mean_ready")
        rstd_ready, ready, stored = sem("f_rstd_ready"), sem("f_ready"), sem("f_stored")
        block = ctx.enter_context(nc.Block())

        @block.sync
        def _(sp):
            sp.dma_start(g_row[:, :], io["final_g"].partition_broadcast(P)).then_inc(g_loaded, 16)
            for b, name in enumerate(("y_prompt", "y_sample")):
                dst = io[name][0].rearrange("(u j) d -> u j d", j=QT)
                for j in range(0, QT, 2):
                    i = b * QT + j
                    sp.wait_ge(ready, i + 2)
                    sp.dma_start(dst[:, j:j + 2, :], out[:, i:i + 2, :]).then_inc(stored, 16)
            sp.wait_ge(stored, 16 * NT // 2)

        @block.scalar
        def _(act):
            for i in range(NT):
                act.activation(junk[:, i, :], X[:, i, :], ACT.Square, accum_out=ss[:, i:i + 1]).then_inc(squared, 1)

        @block.gpsimd
        def _(pool):
            for b in range(NB):
                pool.wait_ge(mean_ready, b + 1)
                cols = slice(b * QT, (b + 1) * QT)
                pool.tensor_tensor(rstd[:, cols], ms[:, cols], minus_half[:, cols], ALU.pow).then_inc(rstd_ready, 1)

        @block.vector
        def _(dve):
            dve.wait_ge(g_loaded, 16)
            for b in range(NB):
                cols = slice(b * QT, (b + 1) * QT)
                dve.wait_ge(squared, (b + 1) * QT)
                dve.tensor_scalar(ms[:, cols], ss[:, cols], 1.0 / D, RMS_EPS, ALU.mult, ALU.add).then_inc(mean_ready, 1)
                dve.wait_ge(rstd_ready, b + 1)
                for i in range(b * QT, (b + 1) * QT):
                    dve.scalar_tensor_tensor(out[:, i, :], X[:, i, :], rstd[:, i:i + 1], g_row[:, :], ALU.mult,
                                             ALU.mult).then_inc(ready, 1)


def constants(nc, ident, minus_half):
    with nc.semaphore("filled") as filled, nc.Block() as block:
        @block.gpsimd
        def _(pool):
            pool.memset(minus_half[:, :], -0.5).then_inc(filled, 1)
            pool.memset(ident[:, :], 0.0).then_inc(filled, 1)
            pool.wait_ge(filled, 2)
            pool.affine_select(out=ident[:, :], in_=ident[:, :], compare_op=ALU.not_equal, fill=1.0, base=0,
                               pattern=[[-1, P]], channel_multiplier=1).then_inc(filled, 1)
            pool.wait_ge(filled, 3)


def build(nc, io):
    with ExitStack() as ctx:
        X = ctx.enter_context(nc.sbuf_tensor("X", [P, NT, D], F32))
        ident = ctx.enter_context(nc.sbuf_tensor("ident", [P, P], F32))
        minus_half = ctx.enter_context(nc.sbuf_tensor("minus_half", [P, NT], F32))
        constants(nc, ident, minus_half)
        stage_a(nc, io, X, ident, minus_half)
        with ExitStack() as inner:
            def sb(name, shape, dt):
                return inner.enter_context(nc.sbuf_tensor(name, shape, dt))

            keep = {
                "cT": [[sb(f"c{n}T{s}", [P, kt, NB * S], F32R) for s in "hl"] for n, kt in (("q", KQ), ("kv", KKV))],
                "kT": [sb(f"kT{s}", [P, 2, NB, S], F32R) for s in "hl"],
                "gateT": sb("gateT", [P, B_PAIRS, NB * S], F32),
            }
            stage_b_in(nc, io, X, ident, minus_half, keep)
            stage_b_heads(nc, io, X, ident, keep)
        stage_final(nc, io, X, minus_half)


def _alibi():
    import numpy as np

    slopes = (2.0 ** (-8.0 * np.arange(1, 25) / 24)).astype(np.float32).reshape(3, A_HEADS).astype(np.float64)
    grid = np.arange(S).reshape(P, QT).T.reshape(-1)

    def chunk_tokens(c):
        v = grid.reshape(QT, P)
        if c in (0, QT):
            return v.reshape(QT, 8, 16)[:, 0:8:7].transpose(1, 0, 2).reshape(-1)
        return v[:, 32 * c - 16:32 * c + 16].reshape(-1)

    out = np.empty((A_HEADS, P, 8 * P), np.float64)
    bad = -1e30

    def put(at, tq, tk, dil, radius, slope):
        d = np.abs(tq[:, None] - tk[None, :])
        ok = (d % dil == 0) & (d // dil <= radius)
        for h in range(A_HEADS):
            out[h, :, at:at + len(tk)] = np.where(ok, -slope[h] * d, bad) / A_SCALE

    for n, t in enumerate((0, 1, 3)):
        tq = grid.reshape(QT, P)[:, 32 * t:32 * t + 32].reshape(-1)
        tk = np.concatenate([chunk_tokens(t), chunk_tokens(t + 1)])
        put(2 * P * n, tq, tk, 1, 64, slopes[0])
    for g, dil in ((1, 4), (2, 16)):
        put((5 + g) * P, grid[:P], grid[:P], dil, 64, slopes[g])
    return out.astype(np.float32)


def _rope_tables():
    import numpy as np

    inv_freq = (10000.0 ** (-np.arange(0, B_ROPE, 2) / B_ROPE)).astype(np.float32)
    ang = np.arange(S, dtype=np.float32)[:, None] * inv_freq[None, :]
    cos, sin = np.cos(ang), np.sin(ang)
    tok = np.stack([cos.reshape(P, QT, -1), sin.reshape(P, QT, -1)], 1).reshape(P, -1)
    order = np.arange(S).reshape(P, QT).T.reshape(-1)
    dim = np.zeros((P, S), np.float32)
    c, s = cos[order].T, sin[order].T
    dim[B_NOPE:B_QK] = np.concatenate([c, c])
    dim[B_QK:] = np.concatenate([-s, s])
    return tok.astype(np.float32), (dim * B_SCALE).astype(np.float32)


def kernel(**inputs):
    import numpy as np
    import concourse.bacc as bacc
    from concourse.bass_utils import run_bass_kernel_spmd

    f = {k: np.asarray(v) for k, v in inputs.items()}
    a_in = f["a_w_in"][0].reshape(KT, P, 10, A_HEADS, A_DIM).transpose(3, 2, 1, 0, 4)
    arrays = {
        "x_prompt": f["x_prompt"],
        "x_sample": f["x_sample"],
        "norm_g": np.ascontiguousarray(f["norm_g"].reshape(2, KT, P).transpose(0, 2, 1)),
        "a_w_in": np.ascontiguousarray(a_in.reshape(A_HEADS, 10, P, KT * A_DIM)),
        "a_w_out": f["a_w_out"][0].reshape(A_HEADS, P, D),
        "alibi": _alibi(),
    }
    def k_major(w, kt):
        return np.ascontiguousarray(w.reshape(kt, P, -1).transpose(1, 0, 2).reshape(P, -1))

    b_in = f["b_w_in"][0]
    wq = f["b_w_q_up"][0].reshape(CQ, B_HEADS, B_QK)
    wq = np.concatenate([wq, wq[:, :, 80:96], wq[:, :, 64:80]], axis=2).reshape(KQ, P, B_PAIRS, 2 * P)
    wkv = f["b_w_kv_up"][0].reshape(KKV, P, B_PAIRS, 2, 2, B_NOPE).transpose(2, 1, 0, 4, 3, 5)
    rope_tok, rope_dim = _rope_tables()
    arrays.update({
        "g1": np.ascontiguousarray(f["norm_g"][1].reshape(KT, P).T),
        "gq": np.ascontiguousarray(f["b_q_norm_g"][0].reshape(KQ, P).T),
        "gkv": np.ascontiguousarray(f["b_kv_norm_g"][0].reshape(KKV, P).T),
        "b_w_cq": k_major(b_in[:, :CQ], KT),
        "b_w_ckv": k_major(b_in[:, CQ:CQ + CKV + B_ROPE], KT),
        "b_w_gate": np.ascontiguousarray(b_in[:, CQ + CKV + B_ROPE:].reshape(KT, P, KT, P).transpose(2, 1, 0, 3)
                                         .reshape(KT, P, KT * P)),
        "b_w_q": np.ascontiguousarray(wq.transpose(2, 1, 0, 3).reshape(B_PAIRS, P, KQ * 2 * P)),
        "b_w_kv": np.ascontiguousarray(wkv.reshape(B_PAIRS, P, KKV * 2 * P)),
        "b_w_out": f["b_w_out"][0].reshape(B_PAIRS, P, D),
        "final_g": f["final_norm_g"],
        "rope_tok": rope_tok,
        "rope_dim": rope_dim,
    })
    nc = bacc.Bacc("TRN2", target_bir_lowering=False, num_devices=1, dynamic_dma_scratch_size=1024)
    io = {n: nc.dram_tensor(n, a.shape, F32, kind="ExternalInput").ap() for n, a in arrays.items()}
    for n in ("y_prompt", "y_sample"):
        io[n] = nc.dram_tensor(n, (1, S, D), F32, kind="ExternalOutput").ap()
    build(nc, io)
    r = run_bass_kernel_spmd(nc, [arrays], core_ids=[0])
    return r.results[0]["y_prompt"], r.results[0]["y_sample"]
```

```python
from contextlib import ExitStack

import concourse.bass as bass
from concourse import mybir

F32 = mybir.dt.float32
F32R = mybir.dt.float32r
ALU = mybir.AluOpType
ACT = mybir.ActivationFunctionType
AX = mybir.AxisListType

P = 128
D = 1024
KT = D // P
S = 512
NB = 2
QT = S // P
NT = NB * QT
HALF = D // 2
RMS_EPS = 1e-6

A_HEADS = 8
A_DIM = 128
A_SCALE = float(A_DIM) ** -0.5

HI, LO = 0, 1
SPLIT_PRODUCT = ((HI, HI), (HI, LO), (LO, HI))

PROJ = ["q0", "k0", "v0", "q1", "k1", "v1", "gate", "q2", "k2", "v2"]
BLOCKS = ["q0", "k0", "v0", "q1", "k1", "v1", "out0", "out1", "gate", "q2", "k2", "v2"]


OUTPUTS = ["out0", "out1"]


def is_first(h):
    return isinstance(h, int) and h == 0


def is_past(h):
    return isinstance(h, int) and h == A_HEADS


def names(h):
    return PROJ if is_first(h) else OUTPUTS if is_past(h) else BLOCKS


def block_no(h, name):
    return names(h).index(name) + (0 if is_first(h) else h * len(BLOCKS) - 2)


def block_slot(h, name):
    return names(h).index(name) % 2


def proj_no(h, name):
    return h * len(PROJ) + PROJ.index(name)


NORM_TURNS = NB * KT
TURNS = {"v2": 0, "p": 2, "v0": 10, "v1": 12}
TURNS_FIRST = {"v0": 0, "v1": 2}


def turn_no(h, kind, n):
    if is_first(h):
        return NORM_TURNS + TURNS_FIRST[kind] + n
    return h * 14 + NORM_TURNS - 10 + TURNS[kind] + n


SUMS = {"s0": 0, "s1": 4, "out": 6, "s2": 22}
SUMS_FIRST = {"s0": 0, "s1": 4, "s2": 6}
SUMS_PAST = {"out": 0}


def sum_table(h):
    return SUMS_FIRST if is_first(h) else SUMS_PAST if is_past(h) else SUMS


def sum_no(h, kind, n):
    return sum_table(h)[kind] + n + (0 if is_first(h) else h * 24 - 16)


def sum_slot(h, kind, n):
    return (sum_table(h)[kind] + n) % 2


def output_rows(h, name):
    if is_past(h):
        return [(2 * i + half, half, i) for i in range(NT) for half in range(2) if name == OUTPUTS[0]]
    half = int(name[3])
    return [(half * NT + i, half, i) for i in range(NT)]


def turn_slot(h, kind, n):
    return ((TURNS_FIRST if is_first(h) else TURNS)[kind] + n) % 2


def key_chunk(v, c):
    if c in (0, QT):
        return v.rearrange("p (j s w) -> p s j w", j=QT, w=16)[:, 0:8:7]
    return v.rearrange("p (j u) -> p j u", j=QT)[:, :, 32 * c - 16:32 * c + 16]


def block_major(v, ps):
    return v.rearrange("p (t j w) -> p j t w", t=QT, j=QT), ps.rearrange("p (j t w) -> p j t w", t=QT, j=QT)


def chunk_major(v, ps):
    inner = (v[:, P:].rearrange("p (c j w) -> p j c w", c=QT - 1, j=QT),
             ps.rearrange("p (j u) -> p j u", j=QT)[:, :, 16:P - 16].rearrange("p j (c w) -> p j c w", w=32))
    ends = (v[:, 0:P].rearrange("p (s j w) -> p s j w", s=2, j=QT), key_chunk(ps, 0))
    return inner, ends


BETWEEN = {
    ("q0", 0): (("v2", 0), ("v2", 1)),
    ("k0", 0): (("turn", 0, 0), ("turn", 0, 1)),
    ("k0", 1): (("weigh", 0, 0), ("turn", 0, 2), ("weigh", 0, 1), ("turn", 0, 3)),
    ("v0", 0): (("weigh", 0, 2), ("weigh", 0, 3), ("turn", 1, 0), ("turn", 1, 1)),
    ("v0", 1): (("weigh", 1, 0), ("turn", 1, 2), ("weigh", 1, 1), ("turn", 1, 3)),
    ("q1", 0): (("weigh", 1, 2), ("weigh", 1, 3)),
}
GATED = {("v0", 0): 0, ("q1", 0): 1}
DVE_STEPS = 14

CHUNK_QUERIES = {1: ((0, 1), (1, 0)), 2: ((1, 1), (2, 0)), 3: ((2, 1), (3, 0)), 0: ((0, 0), (3, 1))}


def stage_a(nc, io, X, next_ss, ident, minus_half):
    with ExitStack() as ctx:
        def sb(name, shape, dt=F32):
            return ctx.enter_context(nc.sbuf_tensor(name, shape, dt))

        def sem(name):
            return ctx.enter_context(nc.semaphore(name))

        hT = [sb(f"hT{s}", [P, KT, NB * S], F32R) for s in "hl"]
        qk = [sb(f"qk{s}", [P, 2, NB, S], F32R) for s in "hl"]
        val = [sb(f"val{s}", [P, 3, NB, QT, A_DIM], F32R) for s in "hl"]
        vT = sb("vT", [P, NB, S])
        prob = sb("prob", [P, 2, NB, QT, 2 * P])
        pT = [sb(f"pT{s}", [P, 2, S], F32R) for s in "hl"]
        gate = sb("gate", [P, NB, S])
        y = sb("y", [P, S])
        yT = [sb(f"yT{s}", [P, NB, S], F32R) for s in "hl"]
        raw = sb("raw", [P, 2, KT * P])
        w = [sb(f"w{s}", [P, 2, KT * P], F32R) for s in "hl"]
        bias = sb("bias", [P, 8 * P])
        g_col = sb("g_col", [P, KT])
        ss = sb("ss", [P, NT])
        ms = sb("ms", [P, NT])
        rstd = sb("rstd", [P, NT])
        st_blk = sb("st_blk", [P, NB, QT, 2])
        st_tile = sb("st_tile", [P, NB, QT, 2])
        st_dil = sb("st_dil", [P, NB, QT, 2])
        negmax = sb("negmax", [P, 2, NB, QT])
        joint = sb("joint", [P, NB, QT])
        fac = sb("fac", [P, 2, NB, QT])
        den = sb("den", [P, 2, NB, QT])
        wt = sb("wt", [P, 2, NB, QT])
        wt_blk = sb("wt_blk", [P, NB, QT])

        bank = [ctx.enter_context(nc.psum_tensor(f"bankA{i}", [P, S], F32)) for i in range(8)]
        proj_ps, sum_ps, turn_ps, out_ps = bank[0:2], bank[2:4], bank[4:6], bank[6:8]
        norm_ps = turn_ps + sum_ps
        row_ps = sum_ps + out_ps

        x_loaded = [sem(f"x_loaded{b}") for b in range(NB)]
        g_loaded = sem("g_loaded")
        squared = sem("squared")
        mean_ready = sem("mean_ready")
        rstd_ready = sem("rstd_ready")
        x_scaled = sem("x_scaled")
        raw_loaded = [sem(f"raw_loaded{i}") for i in range(2)]
        bias_loaded = sem("bias_loaded")
        w_hi = sem("w_hi")
        w_split = sem("w_split")
        proj_done = [sem(f"proj_done{b}") for b in range(NB)]
        proj_hi = sem("proj_hi")
        proj_taken = [sem(f"proj_taken{b}") for b in range(NB)]
        gate_exp = sem("gate_exp")
        turned = sem("turned")
        turn_hi = sem("turn_hi")
        turn_taken = sem("turn_taken")
        sum_done = sem("sum_done")
        sum_taken = sem("sum_taken")
        negmax_ready = sem("negmax_ready")
        exp_done = sem("exp_done")
        fac_in = sem("fac_in")
        fac_ready = sem("fac_ready")
        prob_ready = sem("prob_ready")
        o_done = sem("o_done")
        y_ready = sem("y_ready")
        y_hi = sem("y_hi")
        y_split = sem("y_split")
        dve_step = sem("dve_step")
        row_squared = sem("row_squared")

        block = ctx.enter_context(nc.Block())
        scaled_x = prob[:].rearrange("p g b t k -> p (g b) (t k)")

        @block.sync
        def _(sp):
            for b, name in enumerate(("x_prompt", "x_sample")):
                src = io[name][0].rearrange("(u j) d -> u j d", j=QT)
                sp.dma_start(X[:, b * QT:(b + 1) * QT, :], src).then_inc(x_loaded[b], 16)
                if b == 0:
                    sp.dma_start(g_col[:, :], io["norm_g"][0]).then_inc(g_loaded, 16)

            def load_block(h, name):
                n = block_no(h, name)
                slot = block_slot(h, name)
                if not (is_first(h) and PROJ.index(name) < 2):
                    sp.wait_ge(w_split, n - 1)
                if name.startswith("out"):
                    half = int(name[3]) * HALF
                    src = io["a_w_out"][bass.ds(h - 1, 1), :, half:half + HALF].rearrange("o p c -> (o p) c")
                    dst = raw[:, slot, 0:HALF]
                else:
                    at = ["q0", "k0", "v0", "q1", "k1", "v1", "q2", "k2", "v2", "gate"].index(name)
                    src = io["a_w_in"][bass.ds(h, 1), at].rearrange("o p c -> (o p) c")
                    dst = raw[:, slot, :]
                sp.dma_start(dst, src).then_inc(raw_loaded[slot], 16)

            def load_bias(h):
                if not is_first(h):
                    sp.wait_ge(sum_taken, sum_no(h, "s0", 0))
                sp.dma_start(bias[:, :], io["alibi"][bass.ds(h, 1)].rearrange("o p c -> (o p) c")
                             ).then_inc(bias_loaded, 16)

            for name in PROJ:
                load_block(0, name)
                if name == "q0":
                    load_bias(0)
            with sp.Fori(1, A_HEADS) as h:
                for n, name in enumerate(BLOCKS):
                    load_block(h, name)
                    if n == 1:
                        load_bias(h)
            load_block(A_HEADS, "out0")
            load_block(A_HEADS, "out1")

        @block.gpsimd
        def _(pool):
            for b in range(NB):
                cols = slice(b * QT, (b + 1) * QT)
                pool.wait_ge(mean_ready, b + 1)
                pool.tensor_tensor(rstd[:, cols], ms[:, cols], minus_half[:, cols], ALU.pow).then_inc(rstd_ready, 1)

        @block.scalar
        def _(act):
            for b in range(NB):
                act.wait_ge(x_loaded[b], 16)
                for j in range(QT):
                    i = b * QT + j
                    act.activation(hT[LO][:, j, :] if b else scaled_x[:, j, :], X[:, i, :], ACT.Square,
                                   accum_out=ss[:, i:i + 1]).then_inc(squared, 1)

            def split_weights(h, name):
                k, slot = names(h).index(name), block_slot(h, name)
                act.wait_ge(raw_loaded[slot], 16 * (k // 2 + 1) if is_first(h) else h * 96 + 16 * (k // 2))
                if k >= 2 and names(h)[k - 2].startswith("out"):
                    half = int(names(h)[k - 2][3])
                    act.wait_ge(sum_done, sum_no(h, "out", (half + 1) * NT - 1) + 1)
                elif k >= 2:
                    act.wait_ge(proj_done[1], proj_no(h, names(h)[k - 2]) + 1)
                elif not is_first(h):
                    act.wait_ge(proj_done[1], h * len(PROJ) - 1 + k)
                act.activation(w[HI][:, slot, :], raw[:, slot, :], ACT.Copy).then_inc(w_hi, 1)

            def turn(h, kind, n, dst):
                at = turn_no(h, kind, n)
                slot = turn_slot(h, kind, n)
                act.wait_ge(turned, at + 1)
                act.activation(dst(slot, HI), turn_ps[slot][:, :], ACT.Copy).then_inc(turn_hi, 1)

            def take(h, name, b):
                n = proj_no(h, name)
                act.wait_ge(proj_done[b], n + 1)
                ps = proj_ps[b][:, :]
                if name[0] in "qk":
                    g = int(name[1])
                    if g:
                        act.wait_ge(sum_done, sum_no(h, f"s{g - 1}", 3 if g == 1 else 1) + 1)
                    elif not is_first(h):
                        act.wait_ge(sum_done, h * 24 - 16)
                    dst = qk[HI][:, "qk".index(name[0]), b, :]
                    if name == "q0":
                        dst, ps = block_major(dst, ps)
                    act.activation(dst, ps, ACT.Copy).then_inc(proj_hi, 1)
                elif name[0] == "v":
                    if name == "v0":
                        (d0, s0), (d1, s1) = chunk_major(vT[:, b, :], ps)
                        act.activation(d0, s0, ACT.Copy)
                        act.activation(d1, s1, ACT.Copy).then_inc(proj_taken[b], 1)
                    else:
                        act.activation(vT[:, b, :], ps, ACT.Copy).then_inc(proj_taken[b], 1)
                else:
                    if not is_first(h):
                        act.wait_ge(y_ready, h * 2)
                    act.activation(gate[:, b, :], ps, ACT.Exp, scale=-1.0).then_inc(gate_exp, 1)

            def exps(h, g, bs):
                for b in bs:
                    act.wait_ge(negmax_ready, h * 3 + 1 + (0 if g == 0 else 1 + b))
                    st = st_blk if g == 0 else st_dil
                    for t in range(QT):
                        ins = act.activation(prob[:, g, b, t, :], prob[:, g, b, t, :], ACT.Exp,
                                             bias=negmax[:, g, b, t:t + 1], scale=A_SCALE,
                                             accum_out=st[:, b, t, 1:2])
                    if not (g == 0 and b == 0):
                        ins.then_inc(exp_done, 1)

            def factors(h):
                act.wait_ge(fac_in, h + 1)
                act.activation(fac[:, :, :, :], fac[:, :, :, :], ACT.Exp, scale=A_SCALE).then_inc(fac_ready, 1)

            for n, name in enumerate(PROJ[:2]):
                split_weights(0, name)
            act.wait_ge(g_loaded, 16)
            act.wait_ge(squared, NT)
            for b in range(NB):
                for k in range(KT):
                    n = b * KT + k
                    act.wait_ge(turned, n + 1)
                    act.activation(hT[HI][:, k, b * S:(b + 1) * S], norm_ps[n % 4][:, :], ACT.Copy,
                                   scale=g_col[:, k:k + 1]).then_inc(turn_hi, 1)

            def next_split(h, name):
                k = names(h).index(name) + 2
                if k < len(names(h)):
                    split_weights(h, names(h)[k])
                else:
                    split_weights(h + 1, BLOCKS[k - len(names(h))])

            def head(h):
                for name in names(h):
                    for b in range(NB):
                        if name in PROJ:
                            take(h, name, b)
                        if not is_first(h):
                            between(h, name, b)
                        if name == "v2" and b == 0:
                            exps(h, 1, [1])
                    if name in ("v0", "v1"):
                        for b in range(NB):
                            turn(h, name, b, lambda slot, part, b=b, g=int(name[1]): val[part][:, g, b])
                    next_split(h, name)
                    if name == "v0":
                        exps(h, 0, [0, 1])
                    if name == "k2":
                        exps(h, 1, [0])
                factors(h)

            def between(h, name, b):
                for step in BETWEEN.get((name, b), ()):
                    if step[0] == "v2":
                        turn(h, "v2", step[1], lambda slot, part, g=step[1]: val[part][:, 2, g])
                    elif step[0] == "turn":
                        turn(h, "p", 4 * step[1] + step[2], lambda slot, part: pT[part][:, slot, :])
                if (name, b) in GATED:
                    yb = GATED[name, b]
                    act.wait_ge(y_ready, h * 2 - 1 + yb)
                    act.activation(yT[HI][:, yb, :], y[:, :], ACT.Copy).then_inc(y_hi, 1)

            head(0)
            with act.Fori(1, A_HEADS) as h:
                head(h)
            for name in ("q0", "k0", "v0", "q1"):
                for b in range(NB):
                    between(A_HEADS, name, b)
            for i in range(NT):
                act.wait_ge(sum_taken, sum_no(A_HEADS, "out", 2 * i + 1) + 1)
                if i >= QT:
                    act.wait_ge(row_squared, i - QT + 1)
                act.activation(scaled_x[:, i % QT, :], X[:, i, :], ACT.Square,
                               accum_out=next_ss[:, i:i + 1]).then_inc(row_squared, 1)

        @block.vector
        def _(dve):
            def rate(b):
                cols = slice(b * QT, (b + 1) * QT)
                dve.wait_ge(squared, (b + 1) * QT)
                dve.tensor_scalar(ms[:, cols], ss[:, cols], 1.0 / D, RMS_EPS, ALU.mult, ALU.add).then_inc(mean_ready, 1)

            def scale(b, c):
                cols = slice(c * HALF, (c + 1) * HALF)
                if b:
                    dve.wait_ge(turned, (c + 1) * KT // 2)
                for j in range(QT):
                    i = b * QT + j
                    ins = dve.tensor_scalar(scaled_x[:, j, cols], X[:, i, cols], rstd[:, i:i + 1], None, ALU.mult)
                ins.then_inc(x_scaled, 1)

            def norm_turn(b, k):
                n = b * KT + k
                cols = slice(b * S, (b + 1) * S)
                dve.wait_ge(turn_hi, n + 1)
                dve.scalar_tensor_tensor(hT[LO][:, k, cols], norm_ps[n % 4][:, :], g_col[:, k:k + 1],
                                         hT[HI][:, k, cols], ALU.mult, ALU.subtract).then_inc(turn_taken, 1)

            rate(0)
            dve.wait_ge(rstd_ready, 1)
            scale(0, 0)
            scale(0, 1)
            dve.wait_ge(g_loaded, 16)
            for k in range(KT):
                norm_turn(0, k)
                if k == 0:
                    rate(1)
                if k == 3:
                    dve.wait_ge(rstd_ready, 2)
                    scale(1, 0)
                    dve.wait_ge(w_hi, 1)
                    dve.tensor_tensor(w[LO][:, 0, :], raw[:, 0, :], w[HI][:, 0, :], ALU.subtract).then_inc(w_split, 1)
            scale(1, 1)
            dve.wait_ge(w_hi, 2)
            dve.tensor_tensor(w[LO][:, 1, :], raw[:, 1, :], w[HI][:, 1, :], ALU.subtract).then_inc(w_split, 1)
            for k in range(KT):
                norm_turn(1, k)

            def split_weights(h, name):
                slot = block_slot(h, name)
                dve.wait_ge(w_hi, block_no(h, name) + 1)
                dve.tensor_tensor(w[LO][:, slot, :], raw[:, slot, :], w[HI][:, slot, :],
                                  ALU.subtract).then_inc(w_split, 1)

            def turn(h, kind, n, dst):
                at = turn_no(h, kind, n)
                slot = turn_slot(h, kind, n)
                dve.wait_ge(turn_hi, at + 1)
                dve.tensor_tensor(dst(slot, LO), turn_ps[slot][:, :], dst(slot, HI),
                                  ALU.subtract).then_inc(turn_taken, 1)

            def chain(ins, h, n):
                ins.then_inc(dve_step, 1)
                dve.wait_ge(dve_step, h * DVE_STEPS + n + 1)

            def take(h, name, b):
                ps = proj_ps[b][:, :]
                if name[0] in "qk":
                    g, which = int(name[1]), "qk".index(name[0])
                    dve.wait_ge(proj_hi, h * 12 + 4 * g + 2 * which + b + 1)
                    hi, lo = qk[HI][:, which, b, :], qk[LO][:, which, b, :]
                    if name == "q0":
                        hi, _ = block_major(hi, ps)
                        lo, ps = block_major(lo, ps)
                    dve.tensor_tensor(lo, ps, hi, ALU.subtract).then_inc(proj_taken[b], 1)
                elif name == "gate":
                    dve.wait_ge(gate_exp, h * 2 + b + 1)
                    gb = gate[:, b, :]
                    chain(dve.tensor_scalar(gb, gb, 1.0, None, ALU.add), h, 1 + 2 * b)
                    chain(dve.reciprocal(gb, gb), h, 2 + 2 * b)
                    dve.tensor_tensor(gb, ps, gb, ALU.mult).then_inc(proj_taken[b], 1)

            def take_scores(h, kind, n):
                at = sum_no(h, kind, n)
                slot = sum_slot(h, kind, n)
                dve.wait_ge(sum_done, at + 1)
                g = int(kind[1])
                if g == 0:
                    b, pair = n // 2, n % 2
                    dst = prob[:, 0, b, 2 * pair:2 * pair + 2, :].rearrange("p t k -> p (t k)")
                    src = bias[:, 2 * P * pair:2 * P * pair + 4 * P]
                    ps = sum_ps[slot][:, :]
                else:
                    dst = prob[:, 1, n, :, (g - 1) * P:g * P]
                    src = bias[:, (5 + g) * P:(6 + g) * P].unsqueeze(1).broadcast_to((P, QT, P))
                    ps = sum_ps[slot][:].rearrange("p (t k) -> p t k", t=QT)
                dve.tensor_tensor(dst, ps, src, ALU.add).then_inc(sum_taken, 1)
                return at

            def maxima(h, g, bs, at, n):
                dve.wait_ge(sum_taken, at + 1)
                st = (st_blk if g == 0 else st_dil)[:, bs, :, 0]
                chain(dve.tensor_reduce(st, prob[:, g, bs, :, :], AX.X, ALU.max), h, n)
                dve.tensor_scalar(negmax[:, g, bs, :], st, -A_SCALE, None, ALU.mult).then_inc(negmax_ready, 1)

            def joint_softmax(h):
                dve.wait_ge(exp_done, (h + 1) * 3)
                for s in range(4):
                    for d in range(4):
                        ins = dve.tensor_copy(st_tile[32 * d:32 * d + 32, :, s, :], st_blk[32 * s:32 * s + 32, :, d, :])
                chain(ins, h, 7)
                chain(dve.tensor_tensor(joint[:], st_tile[:, :, :, 0], st_dil[:, :, :, 0], ALU.max), h, 8)
                dve.tensor_tensor(fac[:, 0], st_tile[:, :, :, 0], joint[:], ALU.subtract)
                dve.tensor_tensor(fac[:, 1], st_dil[:, :, :, 0], joint[:], ALU.subtract).then_inc(fac_in, 1)
                dve.wait_ge(fac_ready, h + 1)
                dve.tensor_tensor(den[:, 0], fac[:, 0], st_tile[:, :, :, 1], ALU.mult)
                chain(dve.tensor_tensor(den[:, 1], fac[:, 1], st_dil[:, :, :, 1], ALU.mult), h, 9)
                chain(dve.tensor_tensor(den[:, 0], den[:, 0], den[:, 1], ALU.add), h, 10)
                chain(dve.reciprocal(den[:, 1], den[:, 0]), h, 11)
                dve.tensor_tensor(wt[:, 0], fac[:, 0], den[:, 1], ALU.mult)
                chain(dve.tensor_tensor(wt[:, 1], fac[:, 1], den[:, 1], ALU.mult), h, 12)
                for s in range(4):
                    for d in range(4):
                        ins = dve.tensor_copy(wt_blk[32 * s:32 * s + 32, :, d], wt[32 * d:32 * d + 32, 0, :, s])
                chain(ins, h, 13)
                for b in range(NB):
                    for g in range(2):
                        for t in range(QT):
                            scale = wt_blk[:, b, t:t + 1] if g == 0 else wt[:, 1, b, t:t + 1]
                            ins = dve.tensor_scalar(prob[:, g, b, t, :], prob[:, g, b, t, :], scale, None, ALU.mult)
                    ins.then_inc(prob_ready, 1)

            def add_output(h, name):
                for k, half, n in output_rows(h, name):
                    at = sum_no(h, "out", k)
                    cols = slice(half * HALF, (half + 1) * HALF)
                    dve.wait_ge(sum_done, at + 1)
                    dve.tensor_tensor(X[:, n, cols], row_ps[k % 4][:, :], X[:, n, cols], ALU.add).then_inc(sum_taken, 1)

            def between(h, name, b):
                for step in BETWEEN.get((name, b), ()):
                    if step[0] == "v2":
                        turn(h, "v2", step[1], lambda slot, part, g=step[1]: val[part][:, 2, g])
                    elif step[0] == "turn":
                        turn(h, "p", 4 * step[1] + step[2], lambda slot, part: pT[part][:, slot, :])
                if (name, b) in GATED:
                    yb = GATED[name, b]
                    dve.wait_ge(o_done, h * 2 - 1 + yb)
                    dve.tensor_tensor(y[:, :], out_ps[yb][:, :], gate[:, yb, :], ALU.mult).then_inc(y_ready, 1)
                    dve.wait_ge(y_hi, h * 2 - 1 + yb)
                    dve.tensor_tensor(yT[LO][:, yb, :], y[:, :], yT[HI][:, yb, :], ALU.subtract).then_inc(y_split, 1)

            def next_split(h, name):
                k = names(h).index(name) + 2
                if k < len(names(h)):
                    split_weights(h, names(h)[k])
                else:
                    split_weights(h + 1, BLOCKS[k - len(names(h))])

            def head(h):
                for name in names(h):
                    if name in OUTPUTS:
                        add_output(h, name)
                    for b in range(NB):
                        if name in PROJ:
                            take(h, name, b)
                        if not is_first(h):
                            between(h, name, b)
                        if (name, b) in (("k2", 1), ("v2", 0)):
                            at = take_scores(h, "s2", 1 - b)
                            maxima(h, 1, slice(1 - b, 2 - b), at, 6 - b)
                    if name == "v0":
                        for n in range(4):
                            at = take_scores(h, "s0", n)
                    if name == "v1":
                        for b in range(NB):
                            take_scores(h, "s1", b)
                    if name in ("v0", "v1"):
                        for b in range(NB):
                            turn(h, name, b, lambda slot, part, b=b, g=int(name[1]): val[part][:, g, b])
                    next_split(h, name)
                    if name == "v0":
                        maxima(h, 0, slice(0, NB), at, 0)
                joint_softmax(h)

            head(0)
            with dve.Fori(1, A_HEADS) as h:
                head(h)
            for name in ("q0", "k0", "v0", "q1"):
                for b in range(NB):
                    between(A_HEADS, name, b)
            for name in ("out0", "out1"):
                add_output(A_HEADS, name)

        @block.tensor
        def _(pe):
            def norm_turns(b):
                for k in range(KT):
                    n = b * KT + k
                    if k % (KT // 2) == 0:
                        pe.wait_ge(x_scaled, 2 * b + k // (KT // 2) + 1)
                    if n >= 4:
                        pe.wait_ge(turn_taken, n - 3)
                    for j in range(QT):
                        ins = pe.transpose(norm_ps[n % 4][:, j * P:(j + 1) * P],
                                           scaled_x[:, j, k * P:(k + 1) * P], ident[:, :])
                    ins.then_inc(turned, 1)

            def project(h, name, b):
                n, p = block_no(h, name), proj_no(h, name)
                slot = block_slot(h, name)
                pe.wait_ge(w_split, n + 1)
                if not (is_first(h) and name == "q0"):
                    pe.wait_ge(proj_taken[b], p)
                last = KT * len(SPLIT_PRODUCT) - 1
                i = 0
                for k in range(KT):
                    if is_first(h) and name == "q0":
                        pe.wait_ge(turn_taken, b * KT + k + 1)
                    for a, c in SPLIT_PRODUCT:
                        ins = pe.matmul(proj_ps[b][:, :], w[a][:, slot, k * P:(k + 1) * P],
                                        hT[c][:, k, b * S:(b + 1) * S], start=(i == 0), stop=(i == last))
                        i += 1
                ins.then_inc(proj_done[b], 1)

            def turn(h, kind, n, tiles):
                at = turn_no(h, kind, n)
                slot = turn_slot(h, kind, n)
                pe.wait_ge(turn_taken, at - 1)
                for i, tile in enumerate(tiles):
                    ins = pe.transpose(turn_ps[slot][:, i * P:(i + 1) * P], tile, ident[:, :])
                ins.then_inc(turned, 1)

            def turn_values(h, g, b, at_head):
                pe.wait_ge(proj_taken[b], proj_no(at_head, f"v{g}") + 1)
                turn(h, f"v{g}", b, [vT[:, b, j * P:(j + 1) * P] for j in range(QT)])

            def turn_probs(h, b, part):
                if part == 0:
                    pe.wait_ge(prob_ready, h * 2 - 1 + b)
                if part < 2:
                    tiles = [prob[:, 0, b, t, half * P:(half + 1) * P]
                             for c in ((1, 2), (3, 0))[part] for t, half in CHUNK_QUERIES[c]]
                else:
                    tiles = [prob[:, 1, b, t, (part - 2) * P:(part - 1) * P] for t in range(QT)]
                turn(h, "p", 4 * b + part, tiles)

            def weigh_values(h, b, part):
                at = turn_no(h, "p", 4 * b + part)
                slot = part % 2
                pe.wait_ge(turn_taken, at + 1)
                o = out_ps[b][:, :]
                if part < 2:
                    for i, c in enumerate(((1, 2), (3, 0))[part]):
                        t0, t1 = (t for t, _ in CHUNK_QUERIES[c])
                        dst = o.rearrange("p (j s w) -> p s j w", j=QT, w=32)[:, t0:t1 + 1:t1 - t0]
                        for m, (a, d) in enumerate(SPLIT_PRODUCT):
                            pe.matmul(dst, val[a][:, 0, b, c, :], pT[d][:, slot, i * 2 * P:(i + 1) * 2 * P],
                                      start=(part == 0 and i == 0 and m == 0), stop=False, skip_group_check=True)
                else:
                    for t in range(QT):
                        for m, (a, d) in enumerate(SPLIT_PRODUCT):
                            ins = pe.matmul(o[:, t * P:(t + 1) * P], val[a][:, part - 1, b, t, :],
                                            pT[d][:, slot, t * P:(t + 1) * P], start=False,
                                            stop=(part == 3 and m == 2), skip_group_check=True)
                    if part == 3:
                        ins.then_inc(o_done, 1)

            def score(h, kind, n):
                at = sum_no(h, kind, n)
                slot = sum_slot(h, kind, n)
                if not (is_first(h) and kind == "s0" and n < 2):
                    pe.wait_ge(sum_taken, at - 1)
                ps = sum_ps[slot][:, :]
                if kind == "s0":
                    b, pair = n // 2, n % 2
                    if n % 2 == 0:
                        pe.wait_ge(proj_taken[b], proj_no(h, "k0") + 1)
                    for i, t in enumerate((2 * pair, 2 * pair + 1)):
                        for half in range(2):
                            c = t + half
                            for m, (x, z) in enumerate(SPLIT_PRODUCT):
                                ins = pe.matmul(ps[:, (2 * i + half) * P:(2 * i + half + 1) * P],
                                                qk[x][:, 0, b, t * P:(t + 1) * P], key_chunk(qk[z][:, 1, b, :], c),
                                                start=(m == 0), stop=(m == 2))
                else:
                    b = n
                    pe.wait_ge(proj_taken[b], proj_no(h, "k" + kind[1]) + 1)
                    for t in range(QT):
                        cols = slice(t * P, (t + 1) * P)
                        for m, (x, z) in enumerate(SPLIT_PRODUCT):
                            ins = pe.matmul(ps[:, cols], qk[x][:, 0, b, cols], qk[z][:, 1, b, cols],
                                            start=(m == 0), stop=(m == 2))
                ins.then_inc(sum_done, 1)

            def output(h, name):
                pe.wait_ge(w_split, block_no(h, OUTPUTS[1] if is_past(h) else name) + 1)
                if name == "out0":
                    pe.wait_ge(y_split, h * 2)
                for k, half, i in output_rows(h, name):
                    at = sum_no(h, "out", k)
                    if k < 2:
                        pe.wait_ge(sum_taken, at - 1)
                    elif k >= 4:
                        pe.wait_ge(sum_taken, at - 3)
                    b, j = divmod(i, QT)
                    for m, (a, c) in enumerate(SPLIT_PRODUCT):
                        ins = pe.matmul(row_ps[k % 4][:, :], yT[a][:, b, j * P:(j + 1) * P],
                                        w[c][:, block_slot(h, f"out{half}"), 0:HALF], start=(m == 0), stop=(m == 2))
                    ins.then_inc(sum_done, 1)

            def between(h, name, b):
                for step in BETWEEN.get((name, b), ()):
                    if step[0] == "v2":
                        turn_values(h, 2, step[1], h - 1)
                    elif step[0] == "turn":
                        turn_probs(h, *step[1:])
                    else:
                        weigh_values(h, *step[1:])

            def head(h):
                for name in names(h):
                    if name in OUTPUTS:
                        output(h, name)
                    for b in range(NB):
                        if is_first(h) and name == "q0":
                            norm_turns(b)
                        if name in PROJ:
                            project(h, name, b)
                        if not is_first(h):
                            between(h, name, b)
                        if (name, b) in (("k2", 1), ("v2", 0)):
                            score(h, "s2", 1 - b)
                    if name == "v0":
                        for n in range(4):
                            score(h, "s0", n)
                    if name == "v1":
                        for b in range(NB):
                            score(h, "s1", b)
                    if name in ("v0", "v1"):
                        for b in range(NB):
                            turn_values(h, int(name[1]), b, h)

            head(0)
            with pe.Fori(1, A_HEADS) as h:
                head(h)
            for name in ("q0", "k0", "v0", "q1"):
                for b in range(NB):
                    between(A_HEADS, name, b)
            for name in ("out0", "out1"):
                output(A_HEADS, name)


B_HEADS = 16
B_PAIRS = B_HEADS // 2
B_NOPE, B_ROPE, B_V = 64, 32, 64
B_QK = B_NOPE + B_ROPE
B_SCALE = float(B_QK) ** -0.5
CQ, CKV = 384, 256
KQ, KKV = CQ // P, CKV // P


def stage_b_in(nc, io, X, ss, ident, minus_half, keep):
    cT, kT, gateT = keep["cT"], keep["kT"], keep["gateT"]
    with ExitStack() as ctx:
        def sb(name, shape, dt=F32):
            return ctx.enter_context(nc.sbuf_tensor(name, shape, dt))

        def sem(name):
            return ctx.enter_context(nc.semaphore(name))

        hT = [sb(f"hTb{s}", [P, KT, NB * S], F32R) for s in "hl"]
        w = [sb(f"wb{s}", [P, KT * CQ], F32R) for s in "hl"]
        scratch = gateT[:].rearrange("p m t -> p (m t)")
        scaled_x = scratch[:, 0:QT * D].rearrange("p (j d) -> p j d", j=QT)
        latent = scratch[:, 0:NT * CQ].rearrange("p (i c) -> p i c", i=NT)
        raw = scratch[:, QT * D:QT * D + KT * CQ]
        graw = sb("graw", [P, 2, KT * P])
        g_col = sb("gb_col", [P, KT])
        gq_col = sb("gq_col", [P, KQ])
        gkv_col = sb("gkv_col", [P, KKV])
        rope_tab = sb("rope_tab", [P, 2, QT, B_ROPE // 2])
        key_rope = scratch[:, 7 * D:8 * D].rearrange("p (i c) -> p i c", i=NT)
        spare = raw[:, KT * (CKV + B_ROPE):]
        rot = spare[:, 0:4 * QT * B_ROPE // 2].rearrange("p (m j c) -> p m j c", m=4, j=QT)
        kr_raw = spare[:, 4 * QT * B_ROPE // 2:4 * QT * B_ROPE // 2 + NT * B_ROPE].rearrange("p (i c) -> p i c", i=NT)
        ms, rstd = sb("msb", [P, NT]), sb("rstdb", [P, NT])
        stat = sb("stat", [P, 3, 2, NT])

        bank = [ctx.enter_context(nc.psum_tensor(f"bankB{i}", [P, S], F32)) for i in range(8)]
        proj_ps, turn_ps = bank[0:4], bank[4:8]

        small_loaded = sem("b_small_loaded")
        next_loaded = sem("b_next_loaded")
        raw_loaded = sem("b_raw_loaded")
        mean_ready = sem("b_mean_ready")
        rstd_ready = sem("b_rstd_ready")
        x_scaled = sem("b_x_scaled")
        turned = sem("b_turned")
        turn_hi = sem("b_turn_hi")
        turn_taken = sem("b_turn_taken")
        w_hi = sem("b_w_hi")
        w_split = sem("b_w_split")
        lat_done = sem("b_lat_done")
        lat_squared = sem("b_lat_squared")
        lat_mean = sem("b_lat_mean")
        lat_rstd = sem("b_lat_rstd")
        lat_taken = sem("b_lat_taken")
        zeroed = sem("b_zeroed")
        rope_step = sem("b_rope_step")
        rope_done = sem("b_rope_done")
        graw_loaded = [sem(f"b_graw_loaded{i}") for i in range(2)]
        g_hi = sem("b_g_hi")
        g_split = sem("b_g_split")
        gate_done = sem("b_gate_done")
        gate_exp = sem("b_gate_exp")
        gate_step = sem("b_gate_step")
        gate_taken = sem("b_gate_taken")

        widths = (CQ, CKV + B_ROPE)
        ktiles = (KQ, KKV)
        TQ, TKV = NORM_TURNS, NORM_TURNS + NB * KQ
        TR = TKV + NB * KKV
        gw = [t[:, 0:2 * KT * P].rearrange("p (s c) -> p s c", s=2) for t in w]

        block = ctx.enter_context(nc.Block())

        @block.sync
        def _(sp):
            for dst, name in ((g_col, "g1"), (gq_col, "gq"), (gkv_col, "gkv")):
                sp.dma_start(dst[:, :], io[name]).then_inc(small_loaded, 16)
            sp.dma_start(rope_tab[:].rearrange("p a j c -> p (a j c)"), io["rope_tok"]).then_inc(small_loaded, 16)
            sp.dma_start(raw[:, :], io["b_w_cq"]).then_inc(raw_loaded, 16)
            for n in range(2):
                sp.dma_start(graw[:, n, :], io["b_w_gate"][n]).then_inc(graw_loaded[n], 16)
            sp.wait_ge(w_split, KT)
            sp.dma_start(raw[:, 0:KT * widths[1]], io["b_w_ckv"]).then_inc(raw_loaded, 16)
            sp.dma_start(keep["raw_kv"][:, :], io["b_w_kv"][0]).then_inc(next_loaded, 16)
            sp.dma_start(keep["raw_q"][:, :], io["b_w_q"][0]).then_inc(next_loaded, 16)
            for n in range(2, KT):
                sp.wait_ge(g_split, n - 1)
                sp.dma_start(graw[:, n % 2, :], io["b_w_gate"][n]).then_inc(graw_loaded[n % 2], 16)
            sp.wait_ge(next_loaded, 32)

        @block.gpsimd
        def _(pool):
            for b in range(NB):
                cols = slice(b * QT, (b + 1) * QT)
                pool.wait_ge(mean_ready, b + 1)
                pool.tensor_tensor(rstd[:, cols], ms[:, cols], minus_half[:, cols], ALU.pow).then_inc(rstd_ready, 1)
            pool.memset(key_rope, 0.0).then_inc(zeroed, 1)
            for n in range(2 * NT):
                c, i = divmod(n, NT)
                pool.wait_ge(lat_mean, n + 1)
                pool.tensor_tensor(stat[:, 2, c, i:i + 1], stat[:, 1, c, i:i + 1], minus_half[:, 0:1],
                                   ALU.pow).then_inc(lat_rstd, 1)

        @block.scalar
        def _(act):
            def split_w(c, k):
                act.wait_ge(raw_loaded, 16 * (c + 1))
                cols = slice(k * widths[c], (k + 1) * widths[c])
                act.activation(w[HI][:, cols], raw[:, cols], ACT.Copy).then_inc(w_hi, 1)

            def turn(n, dst, scale=None):
                act.wait_ge(turned, n + 1)
                if scale is None:
                    act.activation(dst, turn_ps[n % 4][:, :], ACT.Copy).then_inc(turn_hi, 1)
                else:
                    act.activation(dst, turn_ps[n % 4][:, :], ACT.Copy, scale=scale).then_inc(turn_hi, 1)

            act.wait_ge(small_loaded, 64)
            for b in range(NB):
                for k in range(KT):
                    turn(b * KT + k, hT[HI][:, k, b * S:(b + 1) * S], g_col[:, k:k + 1])
                    if b:
                        split_w(0, k)

            def latents(c):
                for i in range(NT):
                    n = c * NT + i
                    act.wait_ge(lat_done, n + 1)
                    ps = proj_ps[n % 4]
                    cols = CQ if c == 0 else CKV
                    act.activation(latent[:, i, 0:cols], ps[:, 0:cols], ACT.Square,
                                   accum_out=stat[:, 0, c, i:i + 1]).then_inc(lat_squared, 1)
                    if c == 0 and i == NT - 1:
                        for k in range(KT):
                            split_w(1, k)
                    if i == NT - 1:
                        for b in range(NB):
                            for k in range(ktiles[c]):
                                turn((TQ, TKV)[c] + b * ktiles[c] + k,
                                     cT[c][HI][:, k, b * S:(b + 1) * S], (gq_col, gkv_col)[c][:, k:k + 1])

            latents(0)
            latents(1)
            for b in range(NB):
                n = TR + b
                act.wait_ge(turned, n + 1)
                for par in range(2):
                    ins = act.activation(kT[HI][B_NOPE:B_QK, par, b, :], turn_ps[n % 4][B_NOPE:B_QK, :], ACT.Copy)
                ins.then_inc(turn_hi, 1)

            def split_gate(n):
                act.wait_ge(graw_loaded[n % 2], 16 * (n // 2 + 1))
                if n < 2:
                    act.wait_ge(lat_done, 2 * NT)
                else:
                    act.wait_ge(gate_done, 2 * (n - 1))
                act.activation(gw[HI][:, n % 2, :], graw[:, n % 2, :], ACT.Copy).then_inc(g_hi, 1)

            split_gate(0)
            split_gate(1)
            act.wait_ge(turned, TR + NB)
            for n in range(KT):
                for b in range(NB):
                    act.wait_ge(gate_done, 2 * n + b + 1)
                    act.activation(gateT[:, n, b * S:(b + 1) * S], proj_ps[(2 * n + b) % 4][:, :], ACT.Exp,
                                   scale=-1.0).then_inc(gate_exp, 1)
                if n + 2 < KT:
                    split_gate(n + 2)

        @block.vector
        def _(dve):
            def rate(b):
                cols = slice(b * QT, (b + 1) * QT)
                dve.tensor_scalar(ms[:, cols], ss[:, cols], 1.0 / D, RMS_EPS, ALU.mult, ALU.add).then_inc(mean_ready, 1)

            def scale(b, c):
                cols = slice(c * HALF, (c + 1) * HALF)
                if b:
                    dve.wait_ge(turned, (c + 1) * KT // 2)
                for j in range(QT):
                    i = b * QT + j
                    ins = dve.tensor_scalar(scaled_x[:, j, cols], X[:, i, cols], rstd[:, i:i + 1], None, ALU.mult)
                ins.then_inc(x_scaled, 1)

            def split_w(c, k):
                cols = slice(k * widths[c], (k + 1) * widths[c])
                dve.wait_ge(w_hi, c * KT + k + 1)
                dve.tensor_tensor(w[LO][:, cols], raw[:, cols], w[HI][:, cols], ALU.subtract).then_inc(w_split, 1)

            def turn(n, hi, lo, scale):
                dve.wait_ge(turn_hi, n + 1)
                dve.scalar_tensor_tensor(lo, turn_ps[n % 4][:, :], scale, hi, ALU.mult,
                                         ALU.subtract).then_inc(turn_taken, 1)

            def norm_turn(b, k):
                cols = slice(b * S, (b + 1) * S)
                turn(b * KT + k, hT[HI][:, k, cols], hT[LO][:, k, cols], g_col[:, k:k + 1])

            rate(0)
            dve.wait_ge(rstd_ready, 1)
            scale(0, 0)
            scale(0, 1)
            dve.wait_ge(small_loaded, 64)
            for k in range(KT):
                norm_turn(0, k)
                if k == 0:
                    rate(1)
                if k == 3:
                    dve.wait_ge(rstd_ready, 2)
                    scale(1, 0)
            scale(1, 1)
            for k in range(KT):
                norm_turn(1, k)
                split_w(0, k)

            for c in range(2):
                cols = (CQ, CKV)[c]
                for i in range(NT):
                    n = c * NT + i
                    dve.wait_ge(lat_squared, n + 1)
                    dve.tensor_scalar(stat[:, 1, c, i:i + 1], stat[:, 0, c, i:i + 1], 1.0 / cols, RMS_EPS,
                                      ALU.mult, ALU.add).then_inc(lat_mean, 1)
                    if c == 1:
                        dve.tensor_copy(kr_raw[:, i, :], proj_ps[n % 4][:, CKV:CKV + B_ROPE])
                    dve.wait_ge(lat_rstd, n + 1)
                    dve.tensor_scalar(latent[:, i, 0:cols], proj_ps[n % 4][:, 0:cols], stat[:, 2, c, i:i + 1],
                                      None, ALU.mult).then_inc(lat_taken, 1)
                if c == 0:
                    for k in range(KT):
                        split_w(1, k)
                for b in range(NB):
                    for k in range(ktiles[c]):
                        tok = slice(b * S, (b + 1) * S)
                        turn((TQ, TKV)[c] + b * ktiles[c] + k, cT[c][HI][:, k, tok], cT[c][LO][:, k, tok],
                             (gq_col, gkv_col)[c][:, k:k + 1])
            dve.wait_ge(lat_taken, 2 * NT)
            dve.wait_ge(zeroed, 1)
            half = B_ROPE // 2
            for b in range(NB):
                x1 = kr_raw[:, b * QT:(b + 1) * QT, 0:half]
                x2 = kr_raw[:, b * QT:(b + 1) * QT, half:B_ROPE]
                cos, sin = rope_tab[:, 0], rope_tab[:, 1]
                if b:
                    dve.wait_ge(rope_done, b)
                for m, (x, tab) in enumerate(((x1, cos), (x2, sin), (x1, sin), (x2, cos))):
                    ins = dve.tensor_tensor(rot[:, m], x, tab, ALU.mult)
                ins.then_inc(rope_step, 1)
                dve.wait_ge(rope_step, b + 1)
                dst = key_rope[:, b * QT:(b + 1) * QT]
                dve.tensor_tensor(dst[:, :, B_NOPE:B_NOPE + half], rot[:, 0], rot[:, 1], ALU.subtract)
                dve.tensor_tensor(dst[:, :, B_NOPE + half:B_QK], rot[:, 2], rot[:, 3], ALU.add).then_inc(rope_done, 1)
            for b in range(NB):
                n = TR + b
                dve.wait_ge(turn_hi, n + 1)
                for par in range(2):
                    ins = dve.tensor_tensor(kT[LO][B_NOPE:B_QK, par, b, :], turn_ps[n % 4][B_NOPE:B_QK, :],
                                            kT[HI][B_NOPE:B_QK, par, b, :], ALU.subtract)
                ins.then_inc(turn_taken, 1)

            def split_gate(n):
                dve.wait_ge(g_hi, n + 1)
                dve.tensor_tensor(gw[LO][:, n % 2, :], graw[:, n % 2, :], gw[HI][:, n % 2, :],
                                  ALU.subtract).then_inc(g_split, 1)

            split_gate(0)
            split_gate(1)
            for n in range(KT):
                for b in range(NB):
                    m = 2 * n + b
                    g = gateT[:, n, b * S:(b + 1) * S]
                    dve.wait_ge(gate_exp, m + 1)
                    dve.tensor_scalar(g, g, 1.0, None, ALU.add).then_inc(gate_step, 1)
                    dve.wait_ge(gate_step, 2 * m + 1)
                    dve.reciprocal(g, g).then_inc(gate_step, 1)
                    dve.wait_ge(gate_step, 2 * m + 2)
                    dve.tensor_tensor(g, proj_ps[m % 4][:, :], g, ALU.mult).then_inc(gate_taken, 1)
                if n + 2 < KT:
                    split_gate(n + 2)

        @block.tensor
        def _(pe):
            def turn(n, tiles):
                if n >= 4:
                    pe.wait_ge(turn_taken, n - 3)
                for j, tile in enumerate(tiles):
                    ins = pe.transpose(turn_ps[n % 4][:, j * P:(j + 1) * P], tile, ident[:, :])
                ins.then_inc(turned, 1)

            for b in range(NB):
                for k in range(KT):
                    if k % (KT // 2) == 0:
                        pe.wait_ge(x_scaled, 2 * b + k // (KT // 2) + 1)
                    turn(b * KT + k, [scaled_x[:, j, k * P:(k + 1) * P] for j in range(QT)])

            for c in range(2):
                for i in range(NT):
                    n = c * NT + i
                    if n >= 4:
                        pe.wait_ge(lat_taken, n - 3)
                    if c == 0:
                        pe.wait_ge(turn_taken, (i // QT + 1) * KT)
                    for k in range(KT):
                        pe.wait_ge(w_split, c * KT + k + 1)
                        for m, (a, z) in enumerate(SPLIT_PRODUCT):
                            ins = pe.matmul(proj_ps[n % 4][:, 0:widths[c]], hT[a][:, k, i * P:(i + 1) * P],
                                            w[z][:, k * widths[c]:(k + 1) * widths[c]],
                                            start=(k == 0 and m == 0), stop=(k == KT - 1 and m == 2))
                    ins.then_inc(lat_done, 1)
                for b in range(NB):
                    pe.wait_ge(lat_taken, c * NT + (b + 1) * QT)
                    for k in range(ktiles[c]):
                        turn((TQ, TKV)[c] + b * ktiles[c] + k,
                             [latent[:, b * QT + j, k * P:(k + 1) * P] for j in range(QT)])
            for b in range(NB):
                pe.wait_ge(rope_done, b + 1)
                turn(TR + b, [key_rope[:, b * QT + j, :] for j in range(QT)])
            for n in range(KT):
                pe.wait_ge(g_split, n + 1)
                for b in range(NB):
                    m = 2 * n + b
                    if m >= 4:
                        pe.wait_ge(gate_taken, m - 3)
                    for k in range(KT):
                        for q, (a, z) in enumerate(SPLIT_PRODUCT):
                            ins = pe.matmul(proj_ps[m % 4][:, :], gw[a][:, n % 2, k * P:(k + 1) * P],
                                            hT[z][:, k, b * S:(b + 1) * S], start=(k == 0 and q == 0),
                                            stop=(k == KT - 1 and q == 2))
                    ins.then_inc(gate_done, 1)


UNITS = ((0, 0), (0, 1), (1, 0), (1, 1))


def steps_b(prev, nxt):
    def attend(u, scored, fill, end, extras=(), late=False):
        def at(t):
            return [e for where, e in extras if where == t]

        def own(*steps):
            return [] if u is None else [(kind, u, kb) for kind, kb in steps]

        s = own(("turn", 0), ("turn", 1))
        s += [("score", scored, 0)] + fill if late else fill + [("score", scored, 0)]
        s += [("exp", scored, 0)] + at(0)
        s += [("score", scored, 1)] + own(("weigh", 0), ("turn", 2)) + [("norm", scored, 0), ("exp", scored, 1)] + at(1)
        s += [("score", scored, 2)] + own(("weigh", 1), ("turn", 3)) + [("norm", scored, 1), ("exp", scored, 2)] + at(2)
        s += [("score", scored, 3)] + own(("weigh", 2)) + [("norm", scored, 2), ("exp", scored, 3)] + at(3)
        return s + end + own(("weigh", 3)) + [("norm", scored, 3)]

    def outs(*ns):
        return [("out", n) for n in ns if prev]

    s = [("q_up", 0, 0), ("k_up", 0), ("rope", 0, 0)]
    s += [("fold", -2)] if prev else []
    s += [("q_up", 0, 1)]
    s += [("y", -4)] if prev else []
    s += attend(-1 if prev else None, 0, [("k_up", 1)], [("v_up", 0), ("v_up", 1)],
                [(0, ("rope", 0, 1))] + ([(1, ("y", -3)), (2, ("y", -2))] if prev else []))
    s += [("fold", -1)] if prev else []
    s += [("v_turn", 0), ("q_up", 1, 0), ("v_turn", 1)]
    s += [("y", -1)] if prev else []
    s += [("q_up", 1, 1), ("rope", 1, 0)]
    s += attend(0, 1, outs(0), outs(1),
                [(0, ("rope", 1, 1))] + ([(2, ("split_kv",)), (3, ("split_q",))] if nxt else []), late=True)
    s += outs(2) + [("fold", 0)] + outs(3, 4, 5, 6)
    s += attend(1, 2, outs(7), outs(8), [(2, ("split_out", 0))])
    s += outs(9) + [("fold", 1)] + outs(10, 11, 12, 13)
    s += attend(2, 3, outs(14), outs(15))
    return s + [("split_out", 1)]


LAST_STEPS = [("y", -4), ("y", -3), ("fold", -2), ("turn", -1, 0), ("turn", -1, 1), ("y", -2), ("weigh", -1, 0), ("turn", -1, 2),
              ("weigh", -1, 1), ("turn", -1, 3), ("weigh", -1, 2), ("weigh", -1, 3), ("fold", -1),
              ("y", -1)]
BESIDE = {4: [("rate", 0)], 5: [("scale", 2), ("final", 0)], 6: [("scale", 3), ("final", 1)]}
for i_row in range(NT):
    LAST_STEPS += [("out", i_row), ("out", NT + i_row), ("square", i_row)] + BESIDE.get(i_row, [])
LAST_STEPS += [("rate", 1)] + [("final", i_row) for i_row in range(QT, NT)]
RING = 5
USERS = ("k_up", "q_up", "v_up", "score", "out")
TURNERS = ("turn", "v_turn")


def places(banks, kinds):
    first, each, last = ([s for s in steps if s[0] in kinds]
                         for steps in (steps_b(False, True), steps_b(True, True), LAST_STEPS))
    assert len(each) % banks == 0

    def place(p, step):
        if isinstance(p, int) and p == 0:
            n = first.index(step)
            return n, n % banks, n // banks
        n = (last if isinstance(p, int) and p == B_PAIRS else each).index(step)
        slot = n % banks
        before = len(range(slot, len(first), banks)) - len(each) // banks + n // banks
        return p * len(each) + (len(first) - len(each) + n), slot, p * (len(each) // banks) + before
    return place


ring = places(RING, USERS)
turning = places(2, TURNERS)


def stage_b_heads(nc, io, X, ident, minus_half, keep):
    cT, kT, gateT = keep["cT"], keep["kT"], keep["gateT"]
    with ExitStack() as ctx:
        def sb(name, shape, dt=F32):
            return ctx.enter_context(nc.sbuf_tensor(name, shape, dt))

        def sem(name):
            return ctx.enter_context(nc.semaphore(name))

        qT = [sb(f"qT{s}", [P, 2, NB, S], F32R) for s in "hl"]
        v = sb("v", [P, NB, QT, 2, 2 * B_V], F32R)
        vT = sb("vTb", [P, NB, S])
        prob = sb("probb", [P, 2, QT, S])
        pT = [sb(f"pTb{s}", [P, 2, S], F32R) for s in "hl"]
        o_low = sb("o_low", [P, S])
        y = sb("yb", [P, NB, S])
        yT = [sb(f"yTb{s}", [P, NB, S], F32R) for s in "hl"]
        rope = sb("rope", [P, 2, 2, S])
        table = sb("table", [P, S])
        raw_q, raw_kv, raw_o = keep["raw_q"], keep["raw_kv"], sb("raw_o", [P, HALF])
        wq = [sb(f"wq{s}", [P, KQ * 2 * P], F32R) for s in "hl"]
        wkv = [sb(f"wkv{s}", [P, KKV * 2 * P], F32R) for s in "hl"]
        wo = [sb(f"wo{s}", [P, D], F32R) for s in "hl"]
        negmax = sb("negmaxb", [P, 4, QT])
        total = sb("total", [P, 4, QT])
        inv = sb("inv", [P, 4, QT])

        ss, ms, rstd = sb("ssf", [P, NT]), sb("msf", [P, NT]), sb("rstdf", [P, NT])
        g_row = prob[:, 0, 0:2, :].rearrange("p t c -> p (t c)")
        junk = prob[:, 0, 2:4, :].rearrange("p t c -> p (t c)")

        bank = [ctx.enter_context(nc.psum_tensor(f"bankC{i}", [P, S], F32)) for i in range(8)]
        ring_ps, turn_ps, o_ps = bank[0:RING], bank[5:7], bank[7]

        table_loaded = sem("table_loaded")
        q_loaded, kv_loaded, o_loaded = sem("q_loaded"), sem("kv_loaded"), sem("o_loaded")
        q_w_hi, kv_w_hi, o_w_hi = sem("q_w_hi"), sem("kv_w_hi"), sem("o_w_hi")
        q_w_split, kv_w_split, o_w_split = sem("q_w_split"), sem("kv_w_split"), sem("o_w_split")
        ring_done = sem("ring_done")
        ring_taken = [sem(f"ring_taken{i}") for i in range(RING)]
        k_hi, q_hi = sem("k_hi"), sem("q_hi")
        rope_parts, rope_sum, rope_hi, rope_split = sem("rope_parts"), sem("rope_sum"), sem("rope_hi"), sem("rope_split")
        negmax_ready, inv_ready = sem("negmaxb_ready"), sem("inv_ready")
        prob_ready, last_prob_ready = sem("probb_ready"), sem("last_prob_ready")
        turned, turn_hi, turn_taken = sem("turnedb"), sem("turnb_hi"), sem("turnb_taken")
        o_done, o_copied, o_taken = sem("ob_done"), sem("o_copied"), sem("o_taken")
        y_ready, y_hi, y_split = sem("yb_ready"), sem("yb_hi"), sem("yb_split")

        g_loaded, squared, mean_ready = sem("f_g_loaded"), sem("f_squared"), sem("f_mean_ready")
        rstd_ready, row_ready, row_scaled, stored = sem("f_rstd_ready"), sem("f_row_ready"), sem("f_row_scaled"), sem("f_stored")

        def unit(p, u):
            return p * 4 + u

        def run(body):
            def go(eng):
                body(0, steps_b(False, True))
                with eng.Fori(1, B_PAIRS - 1) as p:
                    body(p, steps_b(True, True))
                body(B_PAIRS - 1, steps_b(True, False))
                body(B_PAIRS, LAST_STEPS)
            return go

        block = ctx.enter_context(nc.Block())

        @block.sync
        def _(sp):
            def load_q(p):
                sp.dma_start(raw_q[:, :], io["b_w_q"][bass.ds(p, 1)].rearrange("o p c -> (o p) c")).then_inc(q_loaded, 16)

            def load_kv(p):
                sp.dma_start(raw_kv[:, :], io["b_w_kv"][bass.ds(p, 1)].rearrange("o p c -> (o p) c")).then_inc(kv_loaded, 16)

            sp.dma_start(table[:, :], io["rope_dim"]).then_inc(table_loaded, 16)

            def body(p, steps):
                for s in steps:
                    if s == ("q_up", 0, 0) and ("split_kv",) in steps:
                        sp.wait_ge(kv_w_split, p + 1)
                        load_kv(p + 1)
                        sp.wait_ge(q_w_split, p + 1)
                        load_q(p + 1)
                    if s[0] == "split_out":
                        half = s[1]
                        if not (isinstance(p, int) and p == 0 and half == 0):
                            sp.wait_ge(o_w_split, 2 * p + half)
                        src = io["b_w_out"][bass.ds(p, 1), :, half * HALF:(half + 1) * HALF]
                        sp.dma_start(raw_o[:, :], src.rearrange("o p c -> (o p) c")).then_inc(o_loaded, 16)

            run(body)(sp)
            sp.wait_ge(turned, turning(B_PAIRS, ("turn", -1, 0))[0] + 1)
            sp.dma_start(g_row, io["final_g"].partition_broadcast(P)).then_inc(g_loaded, 16)
            for b, name in enumerate(("y_prompt", "y_sample")):
                dst = io[name][0].rearrange("(u j) d -> u j d", j=QT)
                for j in range(QT):
                    i = b * QT + j
                    if i in (2, 3):
                        sp.wait_ge(row_scaled, 2 * (i - 1))
                    else:
                        sp.wait_ge(row_ready, i + 1 if i < 2 else i - 1)
                    sp.dma_start(dst[:, j, :], X[:, i, :]).then_inc(stored, 16)
            sp.wait_ge(stored, 16 * NT)

        @block.gpsimd
        def _(pool):
            def split(w, raw, hi, ready, n, cols):
                pool.wait_ge(hi, n)
                pool.tensor_tensor(w[LO][:, cols], raw, w[HI][:, cols], ALU.subtract).then_inc(ready, 1)
                pool.wait_ge(ready, n)

            split(wkv, raw_kv[:, :], kv_w_hi, kv_w_split, 1, slice(0, KKV * 2 * P))

            def body(p, steps):
                for s in steps:
                    if s[0] == "split_kv":
                        split(wkv, raw_kv[:, :], kv_w_hi, kv_w_split, p + 2, slice(0, KKV * 2 * P))
                    elif s[0] == "split_q":
                        split(wq, raw_q[:, :], q_w_hi, q_w_split, p + 2, slice(0, KQ * 2 * P))
                    elif s[0] == "split_out":
                        split(wo, raw_o[:, :], o_w_hi, o_w_split, 2 * p + s[1] + 1,
                              slice(s[1] * HALF, (s[1] + 1) * HALF))
                    elif s[0] == "q_up":
                        hd, b = s[1:]
                        n = unit(p, 2 * hd + b)
                        part = rope[B_NOPE:B_QK, b]
                        pool.wait_ge(rope_parts, n + 1)
                        pool.tensor_tensor(part[:, 0], part[:, 0], part[:, 1], ALU.add).then_inc(rope_sum, 1)
                    elif s[0] == "rope":
                        hd, b = s[1:]
                        n = unit(p, 2 * hd + b)
                        rows = slice(B_NOPE, B_QK)
                        pool.wait_ge(rope_hi, n + 1)
                        pool.tensor_tensor(qT[LO][rows, hd, b, :], rope[rows, b, 0, :], qT[HI][rows, hd, b, :],
                                           ALU.subtract).then_inc(rope_split, 1)
                        pool.wait_ge(rope_split, n + 1)
                    elif s[0] == "norm" and s[2] < QT - 1:
                        u, t = s[1:]
                        n = unit(p, u) * (QT - 1) + t
                        tile = prob[:, u % 2, t, :]
                        pool.wait_ge(inv_ready, unit(p, u) * QT + t + 1)
                        pool.tensor_tensor(tile, tile, inv[:, u, t:t + 1].to_broadcast([P, S]),
                                           ALU.mult).then_inc(prob_ready, 1)
                        pool.wait_ge(prob_ready, n + 1)
                    elif s[0] == "fold":
                        n = unit(p, s[1])
                        hd, b = UNITS[s[1] % 4]
                        rows = slice(hd * B_V, (hd + 1) * B_V)
                        pair = p - 1 if s[1] < 0 else p
                        g = gateT[rows, bass.ds(pair, 1), b * S:(b + 1) * S].rearrange("p o t -> p (o t)")
                        pool.wait_ge(o_taken, n + 1)
                        pool.tensor_tensor(y[rows, b, :], y[rows, b, :], g, ALU.mult).then_inc(y_ready, 1)
                        pool.wait_ge(y_ready, n + 1)
                    elif s[0] == "y":
                        n = unit(p, s[1])
                        hd, b = UNITS[s[1] % 4]
                        rows = slice(hd * B_V, (hd + 1) * B_V)
                        pool.wait_ge(y_hi, n + 1)
                        pool.tensor_tensor(yT[LO][rows, b, :], y[rows, b, :], yT[HI][rows, b, :],
                                           ALU.subtract).then_inc(y_split, 1)
                        pool.wait_ge(y_split, n + 1)
                    elif s[0] == "rate":
                        cols = slice(s[1] * QT, (s[1] + 1) * QT)
                        pool.wait_ge(mean_ready, s[1] + 1)
                        pool.tensor_tensor(rstd[:, cols], ms[:, cols], minus_half[:, cols],
                                           ALU.pow).then_inc(rstd_ready, 1)
                    elif s[0] == "scale":
                        i = s[1]
                        if i == 2:
                            pool.wait_ge(g_loaded, 16)
                        pool.wait_ge(row_scaled, 2 * (i - 2) + 1)
                        pool.tensor_tensor(X[:, i, :], X[:, i, :], g_row, ALU.mult).then_inc(row_scaled, 1)

            run(body)(pool)

        @block.scalar
        def _(act):
            def split(w, raw, loaded, hi, n, cols):
                if loaded is not None:
                    act.wait_ge(loaded[0], loaded[1] * 16)
                act.activation(w[HI][:, cols], raw, ACT.Copy).then_inc(hi, 1)

            split(wq, raw_q[:, :], None, q_w_hi, 1, slice(0, KQ * 2 * P))
            split(wkv, raw_kv[:, :], None, kv_w_hi, 1, slice(0, KKV * 2 * P))

            def body(p, steps):
                for s in steps:
                    if s[0] in USERS:
                        n, slot, _ = ring(p, s)
                        ps = ring_ps[slot]
                    if s[0] == "split_kv":
                        act.wait_ge(ring_done, ring(p, ("v_up", 1))[0] + 1)
                        split(wkv, raw_kv[:, :], (kv_loaded, p + 1), kv_w_hi, p + 2, slice(0, KKV * 2 * P))
                    elif s[0] == "split_q":
                        act.wait_ge(ring_done, ring(p, ("q_up", 1, 1))[0] + 1)
                        split(wq, raw_q[:, :], (q_loaded, p + 1), q_w_hi, p + 2, slice(0, KQ * 2 * P))
                    elif s[0] == "split_out":
                        if not (isinstance(p, int) and p == 0):
                            act.wait_ge(ring_done, ring(p, ("out", (s[1] + 1) * NT - 1))[0] + 1)
                        split(wo, raw_o[:, :], (o_loaded, 2 * p + s[1] + 1), o_w_hi, 2 * p + s[1] + 1,
                              slice(s[1] * HALF, (s[1] + 1) * HALF))
                    elif s[0] == "k_up":
                        act.wait_ge(ring_done, n + 1)
                        for hd in range(2):
                            ins = act.activation(kT[HI][0:B_NOPE, hd, s[1], :],
                                                 ps[hd * B_NOPE:(hd + 1) * B_NOPE, :], ACT.Copy)
                        ins.then_inc(k_hi, 1)
                    elif s[0] == "q_up":
                        hd, b = s[1:]
                        act.wait_ge(ring_done, n + 1)
                        act.activation(qT[HI][0:B_NOPE, hd, b, :], ps[0:B_NOPE, :], ACT.Copy,
                                       scale=B_SCALE).then_inc(q_hi, 1)
                    elif s[0] == "rope":
                        hd, b = s[1:]
                        act.wait_ge(rope_sum, unit(p, 2 * hd + b) + 1)
                        act.activation(qT[HI][B_NOPE:B_QK, hd, b, :], rope[B_NOPE:B_QK, b, 0, :],
                                       ACT.Copy).then_inc(rope_hi, 1)
                    elif s[0] == "v_up":
                        b = s[1]
                        act.wait_ge(ring_done, n + 1)
                        act.activation(vT[:, b, :], ps[:, :], ACT.Copy).then_inc(ring_taken[slot], 1)
                    elif s[0] == "v_turn":
                        b = s[1]
                        n, bank, _ = turning(p, s)
                        act.wait_ge(turned, n + 1)
                        act.activation(v[:, b, :, :, 0:B_V].rearrange("p t h c -> p (t h) c"),
                                       turn_ps[bank][:].rearrange("p (a c) -> p a c", c=B_V),
                                       ACT.Copy).then_inc(turn_hi, 1)
                    elif s[0] == "exp":
                        u, t = s[1:]
                        _, slot, _ = ring(p, ("score", u, t))
                        ps = ring_ps[slot]
                        act.wait_ge(negmax_ready, unit(p, u) * QT + t + 1)
                        act.activation(prob[:, u % 2, t, :], ps[:, :], ACT.Exp, bias=negmax[:, u, t:t + 1],
                                       accum_out=total[:, u, t:t + 1]).then_inc(ring_taken[slot], 1)
                    elif s[0] == "norm" and s[2] == QT - 1:
                        u, t = s[1:]
                        tile = prob[:, u % 2, t, :]
                        act.wait_ge(inv_ready, (unit(p, u) + 1) * QT)
                        act.activation(tile, tile, ACT.Copy, scale=inv[:, u, t:t + 1]).then_inc(last_prob_ready, 1)
                    elif s[0] == "turn":
                        u, kb = s[1:]
                        act.wait_ge(turned, turning(p, s)[0] + 1)
                        act.activation(pT[HI][:, kb % 2, :], turn_ps[turning(p, s)[1]][:, :], ACT.Copy).then_inc(turn_hi, 1)
                    elif s[0] == "fold":
                        N = unit(p, s[1])
                        hd, b = UNITS[s[1] % 4]
                        rows = slice(hd * B_V, (hd + 1) * B_V)
                        act.wait_ge(o_done, N + 1)
                        act.activation(o_low[0:B_V, :], o_ps[B_V:2 * B_V, :], ACT.Copy).then_inc(o_copied, 1)
                    elif s[0] == "y":
                        N = unit(p, s[1])
                        hd, b = UNITS[s[1] % 4]
                        rows = slice(hd * B_V, (hd + 1) * B_V)
                        act.wait_ge(y_ready, N + 1)
                        act.activation(yT[HI][rows, b, :], y[rows, b, :], ACT.Copy).then_inc(y_hi, 1)

                    elif s[0] == "square":
                        i = s[1]
                        _, slot, used = ring(p, ("out", NT + i))
                        act.wait_ge(ring_taken[slot], used + 1)
                        if i == 0:
                            act.wait_ge(turned, turning(p, ("turn", -1, 0))[0] + 1)
                        else:
                            act.wait_ge(squared, i)
                        act.activation(junk, X[:, i, :], ACT.Square, accum_out=ss[:, i:i + 1]).then_inc(squared, 1)

                    elif s[0] == "scale":
                        i = s[1]
                        if i == 2:
                            act.wait_ge(rstd_ready, 1)
                        else:
                            act.wait_ge(row_scaled, 2)
                        act.activation(X[:, i, :], X[:, i, :], ACT.Copy, scale=rstd[:, i:i + 1]).then_inc(row_scaled, 1)

            run(body)(act)

        @block.vector
        def _(dve):
            dve.wait_ge(q_w_hi, 1)
            dve.tensor_tensor(wq[LO][:, :], raw_q[:, :], wq[HI][:, :], ALU.subtract).then_inc(q_w_split, 1)
            dve.wait_ge(table_loaded, 16)

            def body(p, steps):
                for s in steps:
                    if s[0] in USERS:
                        n, slot, used = ring(p, s)
                        ps = ring_ps[slot]
                    if s[0] == "k_up":
                        b = s[1]
                        dve.wait_ge(k_hi, p * 2 + b + 1)
                        dve.tensor_tensor(kT[LO][0:B_NOPE, 0, b, :], ps[0:B_NOPE, :], kT[HI][0:B_NOPE, 0, b, :],
                                          ALU.subtract)
                        dve.tensor_tensor(kT[LO][0:B_NOPE, 1, b, :], ps[B_NOPE:2 * B_NOPE, :],
                                          kT[HI][0:B_NOPE, 1, b, :], ALU.subtract).then_inc(ring_taken[slot], 1)
                    elif s[0] == "q_up":
                        hd, b = s[1:]
                        N = unit(p, 2 * hd + b)
                        dve.wait_ge(ring_done, n + 1)
                        if not (isinstance(p, int) and p == 0 and hd == 0):
                            dve.wait_ge(rope_split, N - 1)
                        dve.tensor_tensor(rope[B_NOPE:B_QK, b, 0, :], ps[B_NOPE:B_QK, :], table[B_NOPE:B_QK, :], ALU.mult)
                        dve.tensor_tensor(rope[B_NOPE:B_QK, b, 1, :], ps[B_QK:P, :], table[B_QK:P, :],
                                          ALU.mult).then_inc(rope_parts, 1)
                        dve.wait_ge(q_hi, N + 1)
                        dve.scalar_tensor_tensor(qT[LO][0:B_NOPE, hd, b, :], ps[0:B_NOPE, :], B_SCALE,
                                                 qT[HI][0:B_NOPE, hd, b, :], ALU.mult,
                                                 ALU.subtract).then_inc(ring_taken[slot], 1)
                    elif s[0] == "v_turn":
                        b = s[1]
                        n, bank, _ = turning(p, s)
                        dve.wait_ge(turn_hi, n + 1)
                        dve.tensor_tensor(v[:, b, :, :, B_V:2 * B_V].rearrange("p t h c -> p (t h) c"),
                                          turn_ps[bank][:].rearrange("p (a c) -> p a c", c=B_V),
                                          v[:, b, :, :, 0:B_V].rearrange("p t h c -> p (t h) c"),
                                          ALU.subtract).then_inc(turn_taken, 1)
                    elif s[0] == "score":
                        u, t = s[1:]
                        dve.wait_ge(ring_done, n + 1)
                        dve.tensor_reduce(negmax[:, u, t:t + 1], ps[:, :], AX.X, ALU.max,
                                          negate=True).then_inc(negmax_ready, 1)
                    elif s[0] == "norm":
                        u, t = s[1:]
                        _, slot, used = ring(p, ("score", u, t))
                        dve.wait_ge(ring_taken[slot], used + 1)
                        dve.reciprocal(inv[:, u, t:t + 1], total[:, u, t:t + 1]).then_inc(inv_ready, 1)
                    elif s[0] == "turn":
                        u, kb = s[1:]
                        dve.wait_ge(turn_hi, turning(p, s)[0] + 1)
                        dve.tensor_tensor(pT[LO][:, kb % 2, :], turn_ps[turning(p, s)[1]][:, :], pT[HI][:, kb % 2, :],
                                          ALU.subtract).then_inc(turn_taken, 1)
                    elif s[0] == "fold":
                        N = unit(p, s[1])
                        hd, b = UNITS[s[1] % 4]
                        rows = slice(hd * B_V, (hd + 1) * B_V)
                        dve.wait_ge(o_copied, N + 1)
                        dve.tensor_tensor(y[rows, b, :], o_ps[0:B_V, :], o_low[0:B_V, :], ALU.add).then_inc(o_taken, 1)
                    elif s[0] == "out":
                        half, i = divmod(s[1], NT)
                        cols = slice(half * HALF, (half + 1) * HALF)
                        dve.wait_ge(ring_done, n + 1)
                        dve.tensor_tensor(X[:, i, cols], ps[:, :], X[:, i, cols], ALU.add).then_inc(ring_taken[slot], 1)

                    elif s[0] == "rate":
                        b = s[1]
                        cols = slice(b * QT, (b + 1) * QT)
                        dve.wait_ge(squared, (b + 1) * QT)
                        dve.tensor_scalar(ms[:, cols], ss[:, cols], 1.0 / D, RMS_EPS, ALU.mult,
                                          ALU.add).then_inc(mean_ready, 1)
                        dve.wait_ge(rstd_ready, b + 1)
                        dve.wait_ge(g_loaded, 16)
                    elif s[0] == "final":
                        i = s[1]
                        dve.scalar_tensor_tensor(X[:, i, :], X[:, i, :], rstd[:, i:i + 1], g_row, ALU.mult,
                                                 ALU.mult).then_inc(row_ready, 1)

            run(body)(dve)

        @block.tensor
        def _(pe):
            def free_turning(p, s):
                n, _, used = turning(p, s)
                if not (isinstance(p, int) and p == 0 and used == 0):
                    pe.wait_ge(turn_taken, n - 1)

            def body(p, steps):
                first = isinstance(p, int) and p == 0
                for s in steps:
                    if s[0] in USERS:
                        n, slot, used = ring(p, s)
                        ps = ring_ps[slot]
                        if not (first and used == 0):
                            pe.wait_ge(ring_taken[slot], used)
                    if s[0] == "k_up":
                        b = s[1]
                        pe.wait_ge(kv_w_split, p + 1)
                        for k in range(KKV):
                            for m, (a, z) in enumerate(SPLIT_PRODUCT):
                                ins = pe.matmul(ps[:, :], wkv[a][:, k * 2 * P:k * 2 * P + P],
                                                cT[1][z][:, k, b * S:(b + 1) * S],
                                                start=(k == 0 and m == 0), stop=(k == KKV - 1 and m == 2))
                        ins.then_inc(ring_done, 1)
                    elif s[0] == "q_up":
                        hd, b = s[1:]
                        pe.wait_ge(q_w_split, p + 1)
                        for k in range(KQ):
                            for m, (a, z) in enumerate(SPLIT_PRODUCT):
                                ins = pe.matmul(ps[:, :], wq[a][:, (2 * k + hd) * P:(2 * k + hd + 1) * P],
                                                cT[0][z][:, k, b * S:(b + 1) * S],
                                                start=(k == 0 and m == 0), stop=(k == KQ - 1 and m == 2))
                        ins.then_inc(ring_done, 1)
                    elif s[0] == "v_up":
                        b = s[1]
                        for k in range(KKV):
                            for m, (a, z) in enumerate(SPLIT_PRODUCT):
                                ins = pe.matmul(ps[:, :], wkv[a][:, k * 2 * P + P:(k + 1) * 2 * P],
                                                cT[1][z][:, k, b * S:(b + 1) * S],
                                                start=(k == 0 and m == 0), stop=(k == KKV - 1 and m == 2))
                        ins.then_inc(ring_done, 1)
                    elif s[0] == "score":
                        u, t = s[1:]
                        hd, b = UNITS[u]
                        if t == 0:
                            pe.wait_ge(rope_split, unit(p, u) + 1)
                        for m, (a, z) in enumerate(SPLIT_PRODUCT):
                            if t == 0 and z == LO:
                                _, k_slot, k_used = ring(p, ("k_up", b))
                                pe.wait_ge(ring_taken[k_slot], k_used + 1)
                            if t == 0 and a == LO:
                                _, q_slot, q_used = ring(p, ("q_up", hd, b))
                                pe.wait_ge(ring_taken[q_slot], q_used + 1)
                            ins = pe.matmul(ps[:, :], qT[a][0:B_QK, hd, b, t * P:(t + 1) * P], kT[z][0:B_QK, hd, b, :],
                                            start=(m == 0), stop=(m == 2))
                        ins.then_inc(ring_done, 1)
                    elif s[0] == "turn":
                        u, kb = s[1:]
                        free_turning(p, s)
                        if kb == 0:
                            pe.wait_ge(prob_ready, (unit(p, u) + 1) * (QT - 1))
                            pe.wait_ge(last_prob_ready, unit(p, u) + 1)
                        bank = turning(p, s)[1]
                        for t in range(QT):
                            ins = pe.transpose(turn_ps[bank][:, t * P:(t + 1) * P],
                                               prob[:, u % 2, t, kb * P:(kb + 1) * P], ident[:, :])
                        ins.then_inc(turned, 1)
                    elif s[0] == "v_turn":
                        b = s[1]
                        free_turning(p, s)
                        _, slot, used = ring(p, ("v_up", b))
                        pe.wait_ge(ring_taken[slot], used + 1)
                        bank = turning(p, s)[1]
                        for t in range(QT):
                            ins = pe.transpose(turn_ps[bank][:, t * P:(t + 1) * P], vT[:, b, t * P:(t + 1) * P],
                                               ident[:, :])
                        ins.then_inc(turned, 1)
                    elif s[0] == "weigh":
                        u, kb = s[1:]
                        N = unit(p, u)
                        hd, b = UNITS[u % 4]
                        pe.wait_ge(turn_taken, turning(p, ("turn", u, kb))[0] + 1)
                        if kb == 0 and not (first and u == 0):
                            pe.wait_ge(o_taken, N)
                        for part in (HI, LO):
                            ins = pe.matmul(o_ps[:, :], v[:, b, kb, hd, :], pT[part][:, kb % 2, :],
                                            start=(kb == 0 and part == HI), stop=(kb == 3 and part == LO))
                        if kb == 3:
                            ins.then_inc(o_done, 1)
                    elif s[0] == "out":
                        half, i = divmod(s[1], NT)
                        b, j = divmod(i, QT)
                        if s[1] == 0:
                            pe.wait_ge(y_split, unit(p, 0))
                        if i == 0:
                            pe.wait_ge(o_w_split, 2 * p - 1 + half)
                        for m, (a, z) in enumerate(SPLIT_PRODUCT):
                            ins = pe.matmul(ps[:, :], yT[a][:, b, j * P:(j + 1) * P],
                                            wo[z][:, half * HALF:(half + 1) * HALF], start=(m == 0), stop=(m == 2))
                        ins.then_inc(ring_done, 1)

            run(body)(pe)


def constants(nc, ident, minus_half):
    with nc.semaphore("filled") as filled, nc.Block() as block:
        @block.gpsimd
        def _(pool):
            pool.memset(minus_half[:, :], -0.5).then_inc(filled, 1)
            pool.memset(ident[:, :], 0.0).then_inc(filled, 1)
            pool.wait_ge(filled, 2)
            pool.affine_select(out=ident[:, :], in_=ident[:, :], compare_op=ALU.not_equal, fill=1.0, base=0,
                               pattern=[[-1, P]], channel_multiplier=1).then_inc(filled, 1)
            pool.wait_ge(filled, 3)


def build(nc, io):
    with ExitStack() as ctx:
        X = ctx.enter_context(nc.sbuf_tensor("X", [P, NT, D], F32))
        ident = ctx.enter_context(nc.sbuf_tensor("ident", [P, P], F32))
        minus_half = ctx.enter_context(nc.sbuf_tensor("minus_half", [P, NT], F32))
        ss = ctx.enter_context(nc.sbuf_tensor("row_ss", [P, NT], F32))
        constants(nc, ident, minus_half)
        stage_a(nc, io, X, ss, ident, minus_half)
        with ExitStack() as inner:
            def sb(name, shape, dt):
                return inner.enter_context(nc.sbuf_tensor(name, shape, dt))

            keep = {
                "cT": [[sb(f"c{n}T{s}", [P, kt, NB * S], F32R) for s in "hl"] for n, kt in (("q", KQ), ("kv", KKV))],
                "kT": [sb(f"kT{s}", [P, 2, NB, S], F32R) for s in "hl"],
                "gateT": sb("gateT", [P, B_PAIRS, NB * S], F32),
                "raw_kv": sb("raw_kv", [P, KKV * 2 * P], F32),
                "raw_q": sb("raw_q", [P, KQ * 2 * P], F32),
            }
            stage_b_in(nc, io, X, ss, ident, minus_half, keep)
            stage_b_heads(nc, io, X, ident, minus_half, keep)


def _alibi():
    import numpy as np

    slopes = (2.0 ** (-8.0 * np.arange(1, 25) / 24)).astype(np.float32).reshape(3, A_HEADS).astype(np.float64)
    grid = np.arange(S).reshape(P, QT).T.reshape(-1)

    def chunk_tokens(c):
        v = grid.reshape(QT, P)
        if c in (0, QT):
            return v.reshape(QT, 8, 16)[:, 0:8:7].transpose(1, 0, 2).reshape(-1)
        return v[:, 32 * c - 16:32 * c + 16].reshape(-1)

    out = np.empty((A_HEADS, P, 8 * P), np.float64)
    bad = -1e30

    def put(at, tq, tk, dil, radius, slope):
        d = np.abs(tq[:, None] - tk[None, :])
        ok = (d % dil == 0) & (d // dil <= radius)
        for h in range(A_HEADS):
            out[h, :, at:at + len(tk)] = np.where(ok, -slope[h] * d, bad) / A_SCALE

    for n, t in enumerate((0, 1, 3)):
        tq = grid.reshape(QT, P)[:, 32 * t:32 * t + 32].reshape(-1)
        tk = np.concatenate([chunk_tokens(t), chunk_tokens(t + 1)])
        put(2 * P * n, tq, tk, 1, 64, slopes[0])
    for g, dil in ((1, 4), (2, 16)):
        put((5 + g) * P, grid[:P], grid[:P], dil, 64, slopes[g])
    return out.astype(np.float32)


def _rope_tables():
    import numpy as np

    inv_freq = (10000.0 ** (-np.arange(0, B_ROPE, 2) / B_ROPE)).astype(np.float32)
    ang = np.arange(S, dtype=np.float32)[:, None] * inv_freq[None, :]
    cos, sin = np.cos(ang), np.sin(ang)
    tok = np.stack([cos.reshape(P, QT, -1), sin.reshape(P, QT, -1)], 1).reshape(P, -1)
    order = np.arange(S).reshape(P, QT).T.reshape(-1)
    dim = np.zeros((P, S), np.float32)
    c, s = cos[order].T, sin[order].T
    dim[B_NOPE:B_QK] = np.concatenate([c, c])
    dim[B_QK:] = np.concatenate([-s, s])
    return tok.astype(np.float32), (dim * B_SCALE).astype(np.float32)


def kernel(**inputs):
    import numpy as np
    import concourse.bacc as bacc
    from concourse.bass_utils import run_bass_kernel_spmd

    f = {k: np.asarray(v) for k, v in inputs.items()}
    a_in = f["a_w_in"][0].reshape(KT, P, 10, A_HEADS, A_DIM).transpose(3, 2, 1, 0, 4)
    arrays = {
        "x_prompt": f["x_prompt"],
        "x_sample": f["x_sample"],
        "norm_g": np.ascontiguousarray(f["norm_g"].reshape(2, KT, P).transpose(0, 2, 1)),
        "a_w_in": np.ascontiguousarray(a_in.reshape(A_HEADS, 10, P, KT * A_DIM)),
        "a_w_out": f["a_w_out"][0].reshape(A_HEADS, P, D),
        "alibi": _alibi(),
    }
    def k_major(w, kt):
        return np.ascontiguousarray(w.reshape(kt, P, -1).transpose(1, 0, 2).reshape(P, -1))

    b_in = f["b_w_in"][0]
    wq = f["b_w_q_up"][0].reshape(CQ, B_HEADS, B_QK)
    wq = np.concatenate([wq, wq[:, :, 80:96], wq[:, :, 64:80]], axis=2).reshape(KQ, P, B_PAIRS, 2 * P)
    wkv = f["b_w_kv_up"][0].reshape(KKV, P, B_PAIRS, 2, 2, B_NOPE).transpose(2, 1, 0, 4, 3, 5)
    rope_tok, rope_dim = _rope_tables()
    arrays.update({
        "g1": np.ascontiguousarray(f["norm_g"][1].reshape(KT, P).T),
        "gq": np.ascontiguousarray(f["b_q_norm_g"][0].reshape(KQ, P).T),
        "gkv": np.ascontiguousarray(f["b_kv_norm_g"][0].reshape(KKV, P).T),
        "b_w_cq": k_major(b_in[:, :CQ], KT),
        "b_w_ckv": k_major(b_in[:, CQ:CQ + CKV + B_ROPE], KT),
        "b_w_gate": np.ascontiguousarray(b_in[:, CQ + CKV + B_ROPE:].reshape(KT, P, KT, P).transpose(2, 1, 0, 3)
                                         .reshape(KT, P, KT * P)),
        "b_w_q": np.ascontiguousarray(wq.transpose(2, 1, 0, 3).reshape(B_PAIRS, P, KQ * 2 * P)),
        "b_w_kv": np.ascontiguousarray(wkv.reshape(B_PAIRS, P, KKV * 2 * P)),
        "b_w_out": f["b_w_out"][0].reshape(B_PAIRS, P, D),
        "final_g": f["final_norm_g"],
        "rope_tok": rope_tok,
        "rope_dim": rope_dim,
    })
    nc = bacc.Bacc("TRN2", target_bir_lowering=False, num_devices=1, dynamic_dma_scratch_size=1024)
    io = {n: nc.dram_tensor(n, a.shape, F32, kind="ExternalInput").ap() for n, a in arrays.items()}
    for n in ("y_prompt", "y_sample"):
        io[n] = nc.dram_tensor(n, (1, S, D), F32, kind="ExternalOutput").ap()
    build(nc, io)
    r = run_bass_kernel_spmd(nc, [arrays], core_ids=[0])
    return r.results[0]["y_prompt"], r.results[0]["y_sample"]
```
